# Optimizing a Trainium2 kernel written in Bass

```python
import jax
import jax.numpy as jnp
from jax import lax
import numpy as np

D_MODEL = 1024
BATCH = 1
SEQ = 256
DEPTH = 1

GRID_W = 64
CTX_LEN = 256
RET_HEADS = 4
RET_QK_DIM = 256
RET_V_DIM = 512
RET_QK_W = RET_HEADS * RET_QK_DIM
RET_V_W = RET_HEADS * RET_V_DIM
RET_CHUNK = 128
CONV_W = D_MODEL
CONV_K = 3
N_BRANCH = 2
N_GROUPS = 4
EXPERTS_PER_GROUP = 8
N_EXPERTS = N_GROUPS * EXPERTS_PER_GROUP
EXPERT_HIDDEN = 512
TOP_K_IN_GROUP = 2
ROPE_BASE = 10000.0
NORM_EPS = 1e-6
GN_EPS = 1e-5

OFF_Q = 0
OFF_K = OFF_Q + RET_QK_W
OFF_V = OFF_K + RET_QK_W
OFF_G = OFF_V + RET_V_W
OFF_CB = OFF_G + RET_V_W
OFF_CC = OFF_CB + CONV_W
OFF_CH = OFF_CC + CONV_W
OFF_GATE = OFF_CH + CONV_W
PROJ_W = OFF_GATE + N_BRANCH * D_MODEL

kernel_name = "hybrid_retention_shortconv_hmoe_dit"

def _rmsnorm(x, w):
    xf = x.astype(jnp.float32)
    y = xf * lax.rsqrt(jnp.mean(xf * xf, axis=-1, keepdims=True) + NORM_EPS)
    return (y * w.astype(jnp.float32)).astype(x.dtype)

def _modulate(h, shift, scale):
    return h * (1 + scale) + shift

def _split_heads(t, n_heads):
    b, l, _ = t.shape
    return t.reshape(b, l, n_heads, -1).transpose(0, 2, 1, 3)

def _rope_axis(u, pos):
    nf = u.shape[-1] // 2
    inv = ROPE_BASE ** (-jnp.arange(nf, dtype=jnp.float32) / nf)
    ang = pos[:, None] * inv[None, :]
    cos = jnp.cos(ang).astype(u.dtype)
    sin = jnp.sin(ang).astype(u.dtype)
    u1, u2 = u[..., :nf], u[..., nf:]
    return jnp.concatenate([u1 * cos - u2 * sin, u1 * sin + u2 * cos], axis=-1)

def _rope_2d(t):
    pos = jnp.arange(t.shape[2])
    row = (pos // GRID_W).astype(jnp.float32)
    col = (pos % GRID_W).astype(jnp.float32)
    half = t.shape[-1] // 2
    return jnp.concatenate([_rope_axis(t[..., :half], row), _rope_axis(t[..., half:], col)], axis=-1)

def _decay_logs(log_decay):
    return jnp.log1p(-jnp.exp(log_decay.astype(jnp.float32)))

def _retention_chunked(q, k, v, log_gamma, s0, strict):
    b, h, l, _ = q.shape
    dv = v.shape[-1]
    n_chunks = l // RET_CHUNK
    idx = jnp.arange(RET_CHUNK, dtype=jnp.float32)
    diff = idx[:, None] - idx[None, :]
    mask = (diff > 0) if strict else (diff >= 0)
    lg = log_gamma[:, None, None]
    intra = jnp.where(mask, jnp.exp(jnp.where(mask, diff, 0.0) * lg), 0.0)
    xi = jnp.exp((idx + 1.0)[None, :] * log_gamma[:, None])[:, :, None]
    zeta = jnp.exp((RET_CHUNK - 1.0 - idx)[None, :] * log_gamma[:, None])[:, :, None]
    chunk_decay = jnp.exp(RET_CHUNK * log_gamma)[:, None, None]

    def to_chunks(t):
        t = t.astype(jnp.float32).reshape(b, h, n_chunks, RET_CHUNK, t.shape[-1])
        return jnp.moveaxis(t, 2, 0)

    def step(state, qkv):
        qc, kc, vc = qkv
        scores = jnp.einsum('bhid,bhjd->bhij', qc, kc) * intra
        out = (jnp.einsum('bhij,bhje->bhie', scores, vc)
               + jnp.einsum('bhid,bhde->bhie', qc * xi, state))
        state = chunk_decay * state + jnp.einsum('bhjd,bhje->bhde', kc * zeta, vc)
        return state, out

    s_final, out = lax.scan(step, s0, (to_chunks(q), to_chunks(k), to_chunks(v)))
    return jnp.moveaxis(out, 0, 2).reshape(b, h, l, dv), s_final

def _bidir_retention(q, k, v, log_gamma, s_f, s_b):
    out_f, _ = _retention_chunked(q, k, v, log_gamma[0], s_f, strict=False)
    flip = lambda t: jnp.flip(t, axis=2)
    out_b, _ = _retention_chunked(flip(q), flip(k), flip(v), log_gamma[1], s_b, strict=True)
    return out_f + flip(out_b)

def _context_states(hc, w_in, log_decay):
    kv = hc @ w_in[:, OFF_K:OFF_G]
    k = _split_heads(kv[..., :RET_QK_W], RET_HEADS).astype(jnp.float32) * RET_QK_DIM ** -0.5
    v = _split_heads(kv[..., RET_QK_W:], RET_HEADS).astype(jnp.float32)
    lg = _decay_logs(log_decay)
    ctx_len = k.shape[2]
    pos = jnp.arange(ctx_len, dtype=jnp.float32)
    w_f = jnp.exp((ctx_len - 1.0 - pos)[None, :] * lg[0][:, None])[:, :, None]
    w_b = jnp.exp(pos[None, :] * lg[1][:, None])[:, :, None]
    s_f = jnp.einsum('bhld,bhle->bhde', k * w_f, v)
    s_b = jnp.einsum('bhld,bhle->bhde', k * w_b, v)
    return s_f, s_b

def _short_conv(u, conv_w, n_rows):
    b, l, ch = u.shape
    seqs = u.reshape(b * n_rows, GRID_W, ch) if n_rows is not None else u
    y = lax.conv_general_dilated(
        seqs, conv_w[:, None, :].astype(u.dtype), window_strides=(1,),
        padding=((CONV_K // 2, CONV_K // 2),),
        dimension_numbers=('NWC', 'WIO', 'NWC'), feature_group_count=ch)
    return y.reshape(b, l, ch)

def _token_mixers(h, w_in, log_decay, gn_w, w_ret_o, conv_w, w_conv_o, w_out, s_f, s_b, n_rows):
    b, l, _ = h.shape
    proj = h @ w_in
    q = _split_heads(proj[..., OFF_Q:OFF_K], RET_HEADS)
    k = _split_heads(proj[..., OFF_K:OFF_V], RET_HEADS) * RET_QK_DIM ** -0.5
    v = _split_heads(proj[..., OFF_V:OFF_G], RET_HEADS)
    if n_rows is not None:
        q, k = _rope_2d(q), _rope_2d(k)
    y = _bidir_retention(q, k, v, _decay_logs(log_decay), s_f, s_b)
    mu = jnp.mean(y, axis=-1, keepdims=True)
    var = jnp.mean(jnp.square(y - mu), axis=-1, keepdims=True)
    y = (y - mu) * lax.rsqrt(var + GN_EPS)
    y = y.transpose(0, 2, 1, 3).reshape(b, l, RET_V_W) * gn_w.astype(jnp.float32)
    y = jax.nn.silu(proj[..., OFF_G:OFF_CB]) * y.astype(h.dtype)
    ret_branch = y @ w_ret_o
    u = _short_conv(proj[..., OFF_CC:OFF_CH] * proj[..., OFF_CH:OFF_GATE], conv_w, n_rows)
    conv_branch = (proj[..., OFF_CB:OFF_CC] * u) @ w_conv_o
    gates = jax.nn.sigmoid(proj[..., OFF_GATE:])
    merged = gates[..., :D_MODEL] * ret_branch + gates[..., D_MODEL:] * conv_branch
    return merged @ w_out

def _hier_moe(h, rg_w, rg_b, re_w, re_b, w13, w2):
    b, l, d = h.shape
    t = h.reshape(-1, d)
    g_logits = (t @ rg_w + rg_b).astype(jnp.float32)
    g_prob = jax.nn.softmax(g_logits, axis=-1)
    g_idx = jnp.argmax(g_logits, axis=-1)
    g_w = jnp.take_along_axis(g_prob, g_idx[:, None], axis=1)
    e_logits = (t @ re_w + re_b).astype(jnp.float32).reshape(-1, N_GROUPS, EXPERTS_PER_GROUP)
    e_logits = jnp.take_along_axis(e_logits, g_idx[:, None, None], axis=1)[:, 0]
    e_prob = jax.nn.softmax(e_logits, axis=-1)
    top_w, top_i = lax.top_k(e_prob, TOP_K_IN_GROUP)
    top_w = top_w / jnp.sum(top_w, axis=-1, keepdims=True)
    expert_id = g_idx[:, None] * EXPERTS_PER_GROUP + top_i
    combine = jnp.sum(jax.nn.one_hot(expert_id, N_EXPERTS, dtype=jnp.float32)
                      * (g_w * top_w)[..., None], axis=1).astype(t.dtype)
    out = jnp.zeros_like(t)
    for e in range(N_EXPERTS):
        hid = t @ w13[e]
        act = jax.nn.silu(hid[:, :EXPERT_HIDDEN]) * hid[:, EXPERT_HIDDEN:]
        out = out + combine[:, e:e + 1] * (act @ w2[e])
    return out.reshape(b, l, d)

def setup_inputs(seed: int = 0) -> dict:
    key = jax.random.key(seed)
    ks = jax.random.split(key, 24)
    nrm = jax.random.normal
    f32 = jnp.float32
    base_decay = -(5.0 + jnp.arange(RET_HEADS, dtype=f32)) * np.float32(np.log(2.0))
    return {
        'x': nrm(ks[0], (BATCH, SEQ, D_MODEL), f32),
        'c': nrm(ks[1], (BATCH, D_MODEL), f32),
        'ctx': nrm(ks[2], (BATCH, CTX_LEN, D_MODEL), f32),
        'c_ctx': nrm(ks[3], (D_MODEL,), f32),
        'w_mod': nrm(ks[4], (DEPTH, D_MODEL, 6 * D_MODEL), f32) * (0.5 * D_MODEL ** -0.5),
        'b_mod': nrm(ks[5], (DEPTH, 6 * D_MODEL), f32) * 0.02,
        'norm1_w': 1.0 + 0.02 * nrm(ks[6], (DEPTH, D_MODEL), f32),
        'norm2_w': 1.0 + 0.02 * nrm(ks[7], (DEPTH, D_MODEL), f32),
        'w_in': nrm(ks[8], (DEPTH, D_MODEL, PROJ_W), f32) * D_MODEL ** -0.5,
        'ret_log_decay': base_decay[None, None, :] + 0.1 * nrm(ks[9], (DEPTH, 2, RET_HEADS), f32),
        'ret_gn_w': 1.0 + 0.02 * nrm(ks[10], (DEPTH, RET_V_W), f32),
        'w_ret_o': nrm(ks[11], (DEPTH, RET_V_W, D_MODEL), f32) * RET_V_W ** -0.5,
        'conv_w': nrm(ks[12], (DEPTH, CONV_K, CONV_W), f32) * CONV_K ** -0.5,
        'w_conv_o': nrm(ks[13], (DEPTH, CONV_W, D_MODEL), f32) * CONV_W ** -0.5,
        'w_out': nrm(ks[14], (DEPTH, D_MODEL, D_MODEL), f32) * D_MODEL ** -0.5,
        'router_group_w': nrm(ks[15], (DEPTH, D_MODEL, N_GROUPS), f32) * D_MODEL ** -0.5,
        'router_group_b': 0.01 * nrm(ks[16], (DEPTH, N_GROUPS), f32),
        'router_expert_w': nrm(ks[17], (DEPTH, D_MODEL, N_EXPERTS), f32) * D_MODEL ** -0.5,
        'router_expert_b': 0.01 * nrm(ks[18], (DEPTH, N_EXPERTS), f32),
        'expert_w13': nrm(ks[19], (DEPTH, N_EXPERTS, D_MODEL, 2 * EXPERT_HIDDEN), f32) * D_MODEL ** -0.5,
        'expert_w2': nrm(ks[20], (DEPTH, N_EXPERTS, EXPERT_HIDDEN, D_MODEL), f32) * EXPERT_HIDDEN ** -0.5,
        'final_norm_w': 1.0 + 0.02 * nrm(ks[21], (D_MODEL,), f32),
    }

def reference(x, c, ctx, c_ctx, w_mod, b_mod, norm1_w, norm2_w, w_in, ret_log_decay, ret_gn_w,
              w_ret_o, conv_w, w_conv_o, w_out, router_group_w, router_group_b, router_expert_w,
              router_expert_b, expert_w13, expert_w2, final_norm_w):
    n_rows = x.shape[1] // GRID_W
    for layer in range(DEPTH):
        mod_x = jnp.split((jax.nn.silu(c) @ w_mod[layer] + b_mod[layer])[:, None, :], 6, axis=-1)
        mod_c = jnp.split(jax.nn.silu(c_ctx) @ w_mod[layer] + b_mod[layer], 6, axis=-1)
        mixer_w = (w_in[layer], ret_log_decay[layer], ret_gn_w[layer], w_ret_o[layer],
                   conv_w[layer], w_conv_o[layer], w_out[layer])
        moe_w = (router_group_w[layer], router_group_b[layer], router_expert_w[layer],
                 router_expert_b[layer], expert_w13[layer], expert_w2[layer])
        hx = _modulate(_rmsnorm(x, norm1_w[layer]), mod_x[0], mod_x[1])
        hc = _modulate(_rmsnorm(ctx, norm1_w[layer]), mod_c[0], mod_c[1])
        s_f, s_b = _context_states(hc, w_in[layer], ret_log_decay[layer])
        x = x + mod_x[2] * _token_mixers(hx, *mixer_w, s_f, s_b, n_rows)
        if layer < DEPTH - 1:
            zero_state = jnp.zeros_like(s_f)
            ctx = ctx + mod_c[2] * _token_mixers(hc, *mixer_w, zero_state, zero_state, None)
            hc2 = _modulate(_rmsnorm(ctx, norm2_w[layer]), mod_c[3], mod_c[4])
            ctx = ctx + mod_c[5] * _hier_moe(hc2, *moe_w)
        hx2 = _modulate(_rmsnorm(x, norm2_w[layer]), mod_x[3], mod_x[4])
        x = x + mod_x[5] * _hier_moe(hx2, *moe_w)
    return _rmsnorm(x, final_norm_w)


_drawn_inputs = setup_inputs


def setup_inputs(seed=0):
    import zlib

    import numpy as np

    out = dict(_drawn_inputs(seed))
    spreads = {}
    factors = {'norm1_w': 5.032,
     'norm2_w': 18.278,
     'ret_gn_w': 64.0,
     'router_group_b': 64.0,
     'router_expert_b': 64.0,
     'final_norm_w': 7.457}
    for name, (base, spread) in spreads.items():
        noise = np.random.default_rng([zlib.crc32(name.encode()), seed]).standard_normal(out[name].shape)
        drawn = base * np.exp(spread * noise) if base else spread * noise
        out[name] = jnp.asarray(drawn.astype(out[name].dtype))
    for name, factor in factors.items():
        out[name] = (out[name] * factor).astype(out[name].dtype)
    return out
```

```python
from contextlib import ExitStack

import numpy as np

import concourse.bass as bass
from concourse import mybir

F32 = mybir.dt.float32
F32R = mybir.dt.float32r
I32 = mybir.dt.int32
ACT = mybir.ActivationFunctionType
ALU = mybir.AluOpType
AX = mybir.AxisListType

P = 128
D = 1024
T = 256
GRID = 64
H = 4
QK = 256
DV = 512
KT = D // P
NE = 32
NG = 4
EPG = 8
HID = 512
CAP = 64
NORM_EPS = 1e-6
GN_EPS = 1e-5
BIG = 3.0e38

W_Q, W_K, W_V, W_G, W_CB, W_CC, W_CH, W_GATE = 0, 2, 4, 8, 12, 14, 16, 18

RAW = 3
HL = 2
HLB = 3

STEPS = ([("TV", 0), ("XT", 0), ("XT", 1), ("XT", 2)]
         + [(k, j) for j in range(4) for k in ("M", "MC")]
         + [("K", 0), ("Q", 0), ("V", 0), ("S", 0), ("G", 0), ("PV", 0), ("V", 1), ("T", 0), ("RO", 0),
            ("S", 1), ("G", 1), ("PV", 1), ("K", 1), ("T", 1), ("RO", 1),
            ("Q", 1), ("V", 2), ("S", 2), ("G", 2), ("PV", 2), ("V", 3), ("T", 2), ("RO", 2),
            ("S", 3), ("G", 3), ("PV", 3), ("CH", 0), ("T", 3), ("RO", 3),
            ("CC", 0), ("CB", 0), ("CH", 1), ("CC", 1), ("CO", 0), ("CB", 1), ("GA", 0), ("CO", 1),
            ("GA", 1), ("GB", 0), ("GB", 1)]
         + [(k, j) for j in (4, 5) for k in ("M", "MB")]
         + [("WO", 0), ("WO", 1)]
         + [(k, j) for j in range(6, 12) for k in ("M", "MB")]
         + [("HT", 0), ("LG", 0), ("PS", 0)])
CHUNKED = ("M", "K", "Q", "V", "G", "RO", "CH", "CC", "CB", "CO", "GA", "GB", "WO")
CHUNKS = [s for s in STEPS if s[0] in CHUNKED]
C0 = len(CHUNKS)
assert C0 % RAW == 0

ACT_KINDS = ("TV", "XT", "M", "K", "V", "S", "G", "PV", "T", "CH", "CB", "GA", "GB", "HT", "LG")
DVE_KINDS = ("TV", "XT", "MC", "MB", "K", "Q", "V", "S", "PV", "T", "RO", "CC", "CB", "CO", "GA", "GB",
             "WO", "HT", "LG", "PS")


def pe_count(step):
    return STEPS.index(step) + 1


def act_count(step):
    return sum(s[0] in ACT_KINDS for s in STEPS[:STEPS.index(step) + 1])


def dve_count(step):
    return sum(s[0] in DVE_KINDS for s in STEPS[:STEPS.index(step) + 1])


def block_kernel(nc, x, c, ctx_in, c_ctx, w_mod, b_mod, norm1_w, norm2_w, w_in, ret_log_decay, ret_gn_w,
                 w_ret_o, conv_w, w_conv_o, w_out, router_group_w, router_group_b, router_expert_w,
                 router_expert_b, expert_w13, expert_w2, final_norm_w, consts, out):
    stack = ExitStack()
    with stack:
        def sem(name):
            return stack.enter_context(nc.semaphore(name))

        BASE = -(-nc.sbuf_base // 64) * 64

        def at(name, kib, shape, dt=F32):
            return nc.alloc_sbuf_tensor_at(name, shape, dt, offset=BASE + int(kib * 1024))

        raw = [at(f"raw{i}", 16 * i, [P, 8, 512]) for i in range(RAW)]
        hi = [at(f"hi{i}", 48 + 16 * i, [P, 8, 512], F32R) for i in range(HL)] + [at("hi2", 128, [P, 8, 512], F32R)]
        lo = [at(f"lo{i}", 80 + 16 * i, [P, 8, 512], F32R) for i in range(HL)] + [at("lo2", 144, [P, 8, 512], F32R)]
        hxh = at("hxh", 112, [P, KT, T], F32R)
        hxl = at("hxl", 120, [P, KT, T], F32R)
        hch = at("hch", 128, [P, KT, T], F32R)
        hcl = at("hcl", 136, [P, KT, T], F32R)
        xtok = at("xtok", 128, [P, 4, D])
        xnT = at("xnT", 144, [P, KT, 2 * T])
        v_sb = at("v_sb", 144, [P, 4, DV])
        racc = at("racc", 152, [P, KT, T])
        cacc = at("cacc", 144, [P, KT, T])
        k_sb = at("k_sb", 160, [P, 4, 2 * T])
        u_sb = at("u_sb", 160, [P, 4, T])
        conv_sb = at("conv_sb", 164, [P, 4, T])
        q_sb = at("q_sb", 168, [P, 4, T])
        ch_sb = at("ch_sb", 168, [P, 4, T])
        att = at("att", 172, [P, 4, T])
        yn = at("yn", 172, [P, 2, DV])
        g_sb = at("g_sb", 176, [P, 4, T])
        yth = at("yth", 180, [P, 4, T], F32R)
        ytl = at("ytl", 184, [P, 4, T], F32R)
        rope = at("rope", 188, [P, 2, 2, T])
        dist = at("dist", 192, [P, 2, T])
        mrow = at("mrow", 194, [5, 2, 512])
        gate1 = at("gate1", 198, [P, D])
        darg = at("darg", 202, [P, 2, T])
        zrow = at("zrow", 202, [1, 512])
        x1 = at("x1", 112, [P, 2, D])
        xres = at("xres", 120, [P, 2, D])
        hx2 = at("hx2", 120, [P, 2, D])
        hx2T = at("hx2T", 160, [P, KT, T])
        shift2 = at("shift2", 168, [P, D])
        scale2 = at("scale2", 176, [P, D])
        norm2 = at("norm2", 180, [P, D])
        xg = at("xg", 160, [P, 2, KT, P], F32R)
        hs = at("hs", 168, [P, 2, HID])
        actp = at("actp", 172, [P, 2, 4, P], F32R)
        yh = at("yh", 176, [P, 2, 512], F32R)
        yl = at("yl", 180, [P, 2, 512], F32R)
        pick = at("pick", 184, [P, 2, P])
        pickw = at("pickw", 185, [P, 2, 2, P])
        am = at("am", 187, [P, 4, CAP])
        sel = at("sel", 188, [P, 2, T], F32R)
        sa = at("sa", 190, [P, 4, CAP])
        posx = at("posx", 191, [P, 2, 4 * NE])
        combx = at("combx", 192, [P, 2, 4 * NE])
        finw = at("finw", 194, [P, D])
        gate2 = at("gate2", 198, [P, D])
        small_at = [204.0]

        def small(name, shape, dt=F32):
            n = 1
            for s in shape[1:]:
                n *= s
            t = at(name, small_at[0], shape, dt)
            small_at[0] += -(-n * 4 // 32) * 32 / 1024
            return t

        ident = small("ident", [P, P])
        tri = at("tri", 193, [P, P])
        ones = at("ones", 193.5, [P, P])
        slot_no = small("slot_no", [P, P])
        vrow = at("vrow", 202, [64, P])
        cols = small("cols", [P, 64])
        csilu = small("csilu", [P, 16])
        cs = small("cs", [P, 8, 4], F32R)
        selc = small("selc", [5, 2])
        modc = small("modc", [P, 16, 2])
        s1 = small("s1", [P, 8, 2])
        lgd = small("lgd", [P, 8])
        lgt = small("lgt", [P, 4, 8])
        stat = small("stat", [P, 4])
        gst = small("gst", [P, 2, 6])
        gmv = small("gmv", [P, 2, 2])
        grs = small("grs", [P, 2])
        cw = small("cw", [P, 2])
        ident2 = small("ident2", [P, CAP])
        desc = small("desc", [P, 8])
        eps = small("eps", [P, 2])
        rmax = small("rmax", [P, 2])
        rounds_i = small("rounds_i", [1, 1], I32)
        rw = at("rw", 172, [P, KT, NG + NE])
        rbias = at("rbias", 174, [P, NG + NE])
        lg = at("lg", 174.25, [P, 2, NG + NE])
        rt = at("rt", 174.75, [P, 2, 96])
        mask = at("mask", 175.5, [P, 2, NE])

        ps = stack.enter_context(nc.psum_tensor("ps", [P, 8, 512], F32))

        landed = [sem(f"landed{i}") for i in range(RAW)]
        hi_done, lo_done, chunk_done = sem("hi_done"), sem("lo_done"), sem("chunk_done")
        pe_step, act_step, dve_step = sem("pe_step"), sem("act_step"), sem("dve_step")
        act_chain, dve_chain = sem("act_chain"), sem("dve_chain")
        in_landed = {n: sem(f"in_{n}") for n in ("consts", "vecs", "x", "ctx", "decay", "xres", "norm2", "router", "finw")}
        brow_landed = [sem(f"brow{i}") for i in range(2)]
        made = sem("constants_made")
        xn_ready, hx_mod, hx_hi, hx_lo = sem("xn_ready"), sem("hx_mod"), sem("hx_hi"), sem("hx_lo")
        squares, roots = sem("squares"), sem("roots")
        darg_ready, decay_ready = sem("darg_ready"), sem("decay_ready")
        gvar_ready, groot_ready = sem("gvar_ready"), sem("groot_ready")
        prod_ready, prod_hi = sem("prod_ready"), sem("prod_hi")
        gates_ready, hx2_ready, logit_ready, exp_ready = (
            sem(n) for n in ("gates_ready", "hx2_ready", "logit_ready", "exp_ready"))
        am_ready = sem("am_ready")
        routed, out_done = sem("routed"), sem("out_done")
        p_ready, pw_ready, g_full, x_hi, x_lo = (sem(n) for n in ("p_ready", "pw_ready", "g_full", "x_hi", "x_lo"))
        h_full, hs_ready, t_full, sa_ready, act_ready = (
            sem(n) for n in ("h_full", "hs_ready", "t_full", "sa_ready", "act_ready"))
        pt_full, sel_ready, cw_ready, y_full, y_hi, y_lo, s_done = (
            sem(n) for n in ("pt_full", "sel_ready", "cw_ready", "y_full", "y_hi", "y_lo", "s_done"))
        fin_ready = sem("fin_ready")

        def k_rows(w, rows=8):
            return w.rearrange("(k p) n -> p k n", p=P)

        w_in_v = k_rows(w_in[0])
        w_mod_v = k_rows(w_mod[0])
        w_out_v = k_rows(w_out[0])
        w_ro_v = w_ret_o[0].rearrange("(h k p) n -> h p k n", k=4, p=P)
        w_co_v = w_conv_o[0].rearrange("(h k p) n -> h p k n", k=4, p=P)
        w13_v = expert_w13[0].rearrange("e (k p) n -> e p k n", p=P)
        w2_v = expert_w2[0].rearrange("e (k p) n -> e p k n", p=P)

        def wide(t):
            return t[:, :, :].rearrange("p (k a) n -> p k (a n)", a=2)

        def col512(v, j):
            return v[:, :, 512 * j:512 * (j + 1)]

        def chunk_source(kind, j):
            at_col = {"K": W_K, "Q": W_Q, "V": W_V, "G": W_G, "CB": W_CB, "CC": W_CC, "CH": W_CH,
                      "GA": W_GATE, "GB": W_GATE + 2}
            if kind == "M":
                return False, col512(w_mod_v, j)
            if kind == "WO":
                return False, col512(w_out_v, j)
            if kind == "RO":
                return True, w_ro_v[j]
            if kind == "CO":
                return True, w_co_v[j]
            return False, col512(w_in_v, at_col[kind] + j)

        class Chain:
            def __init__(self, eng, s):
                self.eng, self.s, self.n = eng, s, 0

            def link(self, ins):
                self.n += 1
                ins.then_inc(self.s, 1)
                self.eng.wait_ge(self.s, self.n)

        def split_hi(eng, raw_slot, lands, part_slot):
            eng.wait_ge(landed[raw_slot], lands)
            for half in range(2):
                k = slice(4 * half, 4 * half + 4)
                eng.activation(hi[part_slot][:, k, :], raw[raw_slot][:, k, :], ACT.Copy).then_inc(hi_done, 1)

        def split_lo(eng, j, raw_slot, part_slot):
            for half in range(2):
                k = slice(4 * half, 4 * half + 4)
                eng.wait_ge(hi_done, 2 * j + half + 1)
                eng.tensor_tensor(lo[part_slot][:, k, :], raw[raw_slot][:, k, :], hi[part_slot][:, k, :],
                                  ALU.subtract).then_inc(lo_done, 1)

        def mixer_slot_free(eng, j):
            if j >= HL:
                eng.wait_ge(pe_step, pe_count(CHUNKS[j - HL]))

        def mixer_hi(eng, j):
            mixer_slot_free(eng, j)
            split_hi(eng, j % RAW, 16 * (j // RAW + 1), j % HL)

        def mixer_lo(eng, j):
            mixer_slot_free(eng, j)
            split_lo(eng, j, j % RAW, j % HL)

        def first_half(i, s):
            return (i, 0) if isinstance(i, int) and i == 0 and s == 0 else (i, 3 * s - 1)

        def second_weights(i, s):
            return (i, 3 * s + 1)

        def number(r, place):
            return C0 + 3 * NE * r + 6 * place[0] + place[1]

        def lands_of(r, place):
            return 16 * (C0 // RAW + NE * r + 2 * place[0] + place[1] // RAW + 1)

        def expert_slot_free(eng, r, place):
            m = number(r, place) - C0
            if isinstance(m, int) and m < HLB:
                eng.wait_ge(pe_step, pe_count(CHUNKS[C0 - 2 + min(m, 1)]))
            else:
                eng.wait_ge(chunk_done, m - HLB + 1)

        def expert_hi(eng, r, place):
            expert_slot_free(eng, r, place)
            split_hi(eng, place[1] % RAW, lands_of(r, place), place[1] % HLB)

        def expert_lo(eng, r, place):
            expert_slot_free(eng, r, place)
            split_lo(eng, number(r, place), place[1] % RAW, place[1] % HLB)

        def nxt(place):
            return place[0], place[1] + 1

        block = stack.enter_context(nc.Block())

        @block.sync
        def _(sp):
            sp.dma_start(vrow[0:8, :], c[0].rearrange("(k p) -> k p", p=P)).then_inc(in_landed["vecs"], 16)
            sp.dma_start(vrow[8:16, :], c_ctx.rearrange("(k p) -> k p", p=P)).then_inc(in_landed["vecs"], 16)
            sp.dma_start(vrow[16:24, :], norm1_w[0].rearrange("(k p) -> k p", p=P)).then_inc(in_landed["vecs"], 16)
            sp.dma_start(vrow[24:40, :], ret_gn_w[0].rearrange("(k p) -> k p", p=P)).then_inc(in_landed["vecs"], 16)
            sp.dma_start(vrow[40:64, :], conv_w[0].rearrange("t (k p) -> (t k) p", p=P)).then_inc(in_landed["vecs"], 16)
            sp.dma_start(xtok[:, 0:2, :], x[0].rearrange("(b p) n -> p b n", p=P)).then_inc(in_landed["x"], 16)
            sp.dma_start(xtok[:, 2:4, :], ctx_in[0].rearrange("(b p) n -> p b n", p=P)).then_inc(in_landed["ctx"], 16)
            for j, (kind, n) in enumerate(CHUNKS):
                if j >= RAW:
                    sp.wait_ge(lo_done, 2 * (j - RAW) + 2)
                wide_chunk, src = chunk_source(kind, n)
                dst = wide(raw[j % RAW]) if wide_chunk else raw[j % RAW][:, :, :]
                sp.dma_start(dst, src).then_inc(landed[j % RAW], 16)

            def load(r, place, src):
                slot = place[1] % RAW
                sp.wait_ge(lo_done, 2 * number(r, place) - 2 * RAW + 2)
                wide_chunk = src.shape[1] == 4
                sp.dma_start(wide(raw[slot]) if wide_chunk else raw[slot][:, :, :], src).then_inc(landed[slot], 16)

            def one_round(r):
                def expert(i, s):
                    e = 2 * i + s
                    p13 = first_half(i, s)
                    load(r, p13, w13_v[e][:, :, 0:512])
                    load(r, nxt(p13), w13_v[e][:, :, 512:1024])
                    if not (isinstance(e, int) and e == 0):
                        load(r, second_weights(i, s), w2_v[e - 1])

                for s in range(2):
                    expert(0, s)
                with sp.Fori(1, NE // 2) as i:
                    for s in range(2):
                        expert(i, s)
                load(r, (NE // 2 - 1, 5), w2_v[NE - 1])

            one_round(0)
            sp.wait_ge(routed, 1)
            rounds = sp.value_load(rounds_i[0:1, 0:1], min_val=1, max_val=4)
            with sp.If(rounds > 1):
                with sp.Fori(1, rounds) as r:
                    one_round(r)
            for b in range(2):
                sp.wait_ge(fin_ready, b + 1)
                sp.dma_start(out[0, b * P:(b + 1) * P, :], hx2[:, b, :]).then_inc(out_done, 16)
            sp.wait_ge(out_done, 32)

        @block.gpsimd
        def _(pool):
            for n, (tile, shape) in enumerate(CONSTS):
                dst = {"ident": ident, "rope": rope, "dist": dist, "slot_no": slot_no, "ident2": ident2, "desc": desc}.get(tile)
                if dst is None:
                    continue
                lo_col = CONST_AT[tile]
                src = consts[:, lo_col:lo_col + shape]
                flat = dst[:] if len(dst.shape) == 2 else dst[:].rearrange(
                    "p a t -> p (a t)" if len(dst.shape) == 3 else "p a b t -> p (a b t)")
                pool.dma_start(flat, src).then_inc(in_landed["consts"], 16)
            pool.dma_start(selc[:, :], consts[0:5, CONST_AT["selc"]:CONST_AT["selc"] + 2]).then_inc(in_landed["consts"], 16)
            pool.dma_start(lgd[:, :], ret_log_decay[0].rearrange("d h -> (d h)").partition_broadcast(P))\
                .then_inc(in_landed["decay"], 16)
            pool.memset(eps[:, 0:1], NORM_EPS)
            pool.memset(eps[:, 1:2], GN_EPS).then_inc(made, 1)
            mods = [s for s in STEPS if s[0] in ("MC", "MB")]
            for j in range(12):
                if j >= 2:
                    pool.wait_ge(pe_step, pe_count(mods[j - 2]))
                pool.dma_start(mrow[4:5, j % 2, :], b_mod[0:1, 512 * j:512 * (j + 1)]).then_inc(brow_landed[j % 2], 16)
                if j == 5:
                    pool.wait_ge(pe_step, pe_count(("GB", 1)))
                    pool.dma_start(xres[:, :, :], x[0].rearrange("(b p) n -> p b n", p=P)).then_inc(in_landed["xres"], 16)
                    pool.wait_ge(dve_step, dve_count(("GB", 1)))
                    pool.wait_ge(act_step, act_count(("GB", 1)))
                    pool.dma_start(norm2[:, :], norm2_w[0].partition_broadcast(P)).then_inc(in_landed["norm2"], 16)
                    pool.dma_start(rw[:, :, 0:NG], router_group_w[0].rearrange("(k p) n -> p k n", p=P)).then_inc(in_landed["router"], 16)
                    pool.dma_start(rw[:, :, NG:], router_expert_w[0].rearrange("(k p) n -> p k n", p=P)).then_inc(in_landed["router"], 16)
                    pool.dma_start(rbias[:, 0:NG], router_group_b[0].partition_broadcast(P)).then_inc(in_landed["router"], 16)
                    pool.dma_start(rbias[:, NG:], router_expert_b[0].partition_broadcast(P)).then_inc(in_landed["router"], 16)
                    pool.dma_start(tri[:, :], consts[:, CONST_AT["tri"]:CONST_AT["tri"] + P]).then_inc(in_landed["router"], 16)
                    pool.dma_start(ones[:, :], consts[:, CONST_AT["ones"]:CONST_AT["ones"] + P]).then_inc(in_landed["router"], 16)
                    pool.memset(zrow[:, :], 0.0).then_inc(made, 1)
            pool.wait_ge(pe_step, pe_count(("MB", 11)))
            pool.dma_start(finw[:, :], final_norm_w.partition_broadcast(P)).then_inc(in_landed["finw"], 16)

        @block.tensor
        def _(pe):
            def after(act=None, dve=None):
                if act is not None:
                    pe.wait_ge(act_step, act_count(act))
                if dve is not None:
                    pe.wait_ge(dve_step, dve_count(dve))

            chunk_no = [0]

            def next_chunk():
                j = chunk_no[0]
                chunk_no[0] += 1
                pe.wait_ge(lo_done, 2 * j + 2)
                return hi[j % HL], lo[j % HL]

            def features_out(wh, wl, banks, operands, rows=8, tiles=4):
                for f in range(tiles):
                    col = slice(f * P, (f + 1) * P)
                    for o, (xh, xl, where) in enumerate(operands):
                        dst = banks(f, o)
                        for k in range(rows):
                            pe.matmul(dst, wh[:, k, col], xh[:, k, :], start=(k == 0), stop=False)
                            pe.matmul(dst, wh[:, k, col], xl[:, k, :], start=False, stop=False)
                            last = pe.matmul(dst, wl[:, k, col], xh[:, k, :], start=False, stop=(k == rows - 1))
                return last

            def tokens_out(dst, stat_h, stat_l, wh, wl):
                for k in range(8):
                    pe.matmul(dst, stat_h(k), wh[:, k, :], start=(k == 0), stop=False)
                    pe.matmul(dst, stat_l(k), wh[:, k, :], start=False, stop=False)
                    last = pe.matmul(dst, stat_h(k), wl[:, k, :], start=False, stop=(k == 7))
                return last

            def half_banks(first):
                return lambda f, o: ps[:, first + f // 2, T * (f % 2):T * (f % 2 + 1)]

            for step in STEPS:
                kind, j = step
                if kind == "TV":
                    pe.wait_ge(in_landed["consts"], 16 * 7)
                    pe.wait_ge(in_landed["vecs"], 16 * 5)
                    last = pe.transpose(ps[:, 5, 0:64], vrow[:, :], ident[0:64, 0:64])
                elif kind == "XT":
                    if j == 0:
                        pe.wait_ge(xn_ready, 4)
                    if j == 1:
                        after(dve=("TV", 0))
                    if j == 2:
                        after(act=("XT", 0), dve=("XT", 0))
                    for k in ((0, 1, 2, 3), (4, 5), (6, 7))[j]:
                        for t in range(4):
                            last = pe.transpose(ps[:, k % 6, t * P:(t + 1) * P], xtok[:, t, k * P:(k + 1) * P], ident[:, :])
                elif kind == "M":
                    wh, wl = next_chunk()
                    if j >= 2:
                        pe.wait_ge(act_step, act_count(("M", j - 1)))
                    if j >= 6:
                        after(dve=("WO", 1))
                    if j == 4:
                        after(act=("GB", 0), dve=("GB", 0))
                    after(act=("TV", 0), dve=("TV", 0))
                    bank = 6 if j < 4 or j >= 6 else 2
                    for k in range(8):
                        pe.matmul(ps[0:4, bank, :], cs[:, k, :], wh[:, k, :], start=(k == 0), stop=False)
                        last = pe.matmul(ps[0:4, bank, :], cs[:, k, :], wl[:, k, :], start=False, stop=(k == 7))
                elif kind == "MC":
                    after(act=("M", j))
                    if j >= 1:
                        after(dve=("MC", j - 1))
                    pe.wait_ge(brow_landed[j % 2], 16 * (j // 2 + 1))
                    for f in range(4):
                        last = pe.matmul(ps[:, 7, 2 * f:2 * f + 2], mrow[0:5, j % 2, f * P:(f + 1) * P], selc[:, :],
                                         start=True, stop=True)
                elif kind == "MB":
                    after(act=("M", j))
                    if j in (5, 7, 8, 9, 10, 11):
                        after(dve=("MB", j - 1))
                    pe.wait_ge(brow_landed[j % 2], 16 * (j // 2 + 1))
                    bank = 7 if j >= 6 else 3
                    last = pe.matmul(ps[:, bank, :], selc[:, 0:1].broadcast_to([5, P]), mrow[0:5, j % 2, :], start=True, stop=True)
                elif kind == "K":
                    wh, wl = next_chunk()
                    if j == 0:
                        after(act=("XT", 2), dve=("MC", 3))
                        pe.wait_ge(hx_lo, 2)
                    else:
                        after(act=("V", 1), dve=("V", 1))
                    last = features_out(wh, wl, lambda f, o: ps[:, f, T * o:T * (o + 1)],
                                        [(hxh, hxl, 0), (hch, hcl, 1)])
                elif kind == "Q":
                    wh, wl = next_chunk()
                    if j == 1:
                        after(dve=("RO", 1))
                    last = features_out(wh, wl, half_banks(4), [(hxh, hxl, 0)])
                elif kind == "V":
                    wh, wl = next_chunk()
                    prev = {0: ("K", 0), 1: ("V", 0), 2: ("K", 1), 3: ("V", 2)}[j]
                    after(act=prev, dve=prev)
                    for t in range(4):
                        sh, sl = (hxh, hxl) if t < 2 else (hch, hcl)
                        b = t % 2
                        last = tokens_out(ps[:, t, :], lambda k: sh[:, k, b * P:(b + 1) * P],
                                          lambda k: sl[:, k, b * P:(b + 1) * P], wh, wl)
                elif kind == "S":
                    after(act=("K", j // 2), dve=("Q", j // 2))
                    if j >= 1:
                        after(dve=("RO", j - 1))
                    for t in range(4):
                        for m in range(2):
                            f = 2 * (j % 2) + m
                            last = pe.matmul(ps[:, 4 + t // 2, T * (t % 2):T * (t % 2 + 1)],
                                             k_sb[:, f, t * P:(t + 1) * P], q_sb[:, f, :], start=(m == 0), stop=(m == 1))
                elif kind == "G":
                    wh, wl = next_chunk()
                    if j >= 1:
                        after(dve=("RO", j - 1))
                    last = features_out(wh, wl, half_banks(6), [(hxh, hxl, 0)])
                elif kind == "PV":
                    after(act=("V", j), dve=("S", j))
                    for b in range(2):
                        for t in range(4):
                            last = pe.matmul(ps[:, 4 + b, :], att[:, t, b * P:(b + 1) * P], v_sb[:, t, :],
                                             start=(t == 0), stop=(t == 3))
                elif kind == "T":
                    after(act=("G", j), dve=("PV", j))
                    for e in range(4):
                        for b in range(2):
                            last = pe.transpose(ps[:, 6 + e // 2, T * (e % 2) + b * P:T * (e % 2) + (b + 1) * P],
                                                yn[:, b, e * P:(e + 1) * P], ident[:, :])
                elif kind in ("RO", "CO"):
                    wh, wl = next_chunk()
                    if kind == "RO":
                        after(dve=("T", j))
                    else:
                        after(dve=("CB", j))
                        after(dve=("RO", 3) if j == 0 else ("CO", 0))
                    last = features_out(wide(wh), wide(wl), half_banks(4), [(yth, ytl, 0)], rows=4, tiles=8)
                elif kind in ("CH", "CC", "CB", "GA", "GB"):
                    wh, wl = next_chunk()
                    first, prev_act, prev_dve = {
                        ("CH", 0): (0, ("K", 1), ("V", 3)), ("CC", 0): (2, ("V", 3), ("V", 3)),
                        ("CB", 0): (0, ("CH", 0), None), ("CH", 1): (0, None, ("CB", 0)),
                        ("CC", 1): (2, None, ("CC", 0)), ("CB", 1): (0, ("CH", 1), None),
                        ("GA", 0): (2, None, ("CC", 1)), ("GA", 1): (0, None, ("CB", 1)),
                        ("GB", 0): (2, ("GA", 0), None), ("GB", 1): (0, ("GA", 1), None)}[step]
                    after(act=prev_act, dve=prev_dve)
                    if step == ("CH", 0):
                        after(act=("V", 3))
                    last = features_out(wh, wl, half_banks(first), [(hxh, hxl, 0)])
                elif kind == "WO":
                    wh, wl = next_chunk()
                    after(dve=("GB", 1))
                    if j == 0:
                        after(dve=("CO", 1))
                    for b in range(2):
                        last = tokens_out(ps[:, 4 + 2 * j + b, :], lambda k: hch[:, k, b * P:(b + 1) * P],
                                          lambda k: hcl[:, k, b * P:(b + 1) * P], wh, wl)
                elif kind == "HT":
                    pe.wait_ge(hx2_ready, 1)
                    after(act=("GB", 1), dve=("MB", 5))
                    for k in range(8):
                        for b in range(2):
                            last = pe.transpose(ps[:, k // 2, T * (k % 2) + b * P:T * (k % 2) + (b + 1) * P],
                                                hx2[:, b, k * P:(k + 1) * P], ident[:, :])
                elif kind == "LG":
                    after(act=("HT", 0), dve=("HT", 0))
                    pe.wait_ge(in_landed["router"], 96)
                    for b in range(2):
                        for k in range(8):
                            last = pe.matmul(ps[:, 4, 64 * b:64 * b + NG + NE], hx2T[:, k, b * P:(b + 1) * P],
                                             rw[:, k, :], start=(k == 0), stop=(k == 7))
                elif kind == "PS":
                    after(dve=("LG", 0))
                    pe.matmul(ps[:, 5, 0:NE], tri[:, :], mask[:, 0, :], start=True, stop=True)
                    pe.matmul(ps[:, 5, NE:2 * NE], tri[:, :], mask[:, 1, :], start=True, stop=False)
                    pe.matmul(ps[:, 5, NE:2 * NE], ones[:, :], mask[:, 0, :], start=False, stop=True)
                    pe.matmul(ps[:, 5, 2 * NE:3 * NE], ones[:, :], mask[:, 0, :], start=True, stop=False)
                    last = pe.matmul(ps[:, 5, 2 * NE:3 * NE], ones[:, :], mask[:, 1, :], start=False, stop=True)
                last.then_inc(pe_step, 1)

            pe.wait_ge(made, 2)
            after(dve=("PS", 0))
            for bank in range(4):
                pe.matmul(ps[:, bank, :], zrow[0:1, 0:P], zrow[0:1, :], start=True, stop=False, skip_group_check=True)

            def one_round(r):
                n0, g0 = NE * r, (NE // 2) * r

                def gather(i):
                    pe.wait_ge(p_ready, g0 + i + 1)
                    for bank in range(2):
                        for k in range(4):
                            f = 4 * bank + k
                            for b in range(2):
                                last = pe.matmul(ps[:, 6 + bank, k * P:(k + 1) * P], hx2[:, b, f * P:(f + 1) * P],
                                                 pick[:, b, :], start=(b == 0), stop=(b == 1))
                        last.then_inc(g_full, 1)

                def first_product(i, s, n):
                    place = first_half(i, s)
                    for half in range(2):
                        j = number(r, place)
                        if half == 0:
                            if s == 0:
                                pe.wait_ge(x_hi, 2 * (g0 + i) + 2)
                                pe.wait_ge(x_lo, 2 * (g0 + i) + 2)
                            if not isinstance(n, int) or n > 0:
                                pe.wait_ge(act_ready, n)
                        elif not isinstance(n, int) or n > 0:
                            pe.wait_ge(sel_ready, n)
                            pe.wait_ge(cw_ready, n)
                        slot = place[1] % HLB
                        for k in range(8):
                            if k % 4 == 0:
                                pe.wait_ge(lo_done, 2 * j + k // 4 + 1)
                            pe.matmul(ps[:, 4 + half, :], xg[:, s, k, :], hi[slot][:, k, :], start=(k == 0), stop=False)
                            last = pe.matmul(ps[:, 4 + half, :], xg[:, s, k, :], lo[slot][:, k, :], start=False,
                                             stop=(k == 7))
                        last.then_inc(chunk_done, 1)
                        place = nxt(place)

                def scatter(n, s):
                    pe.wait_ge(y_lo, 2 * n + 2)
                    pe.wait_ge(sel_ready, n + 1)
                    for b in range(2):
                        for half in range(2):
                            for part in (yh, yl):
                                last = pe.matmul(ps[:, 2 * b + half, :], sel[:, s, b * P:(b + 1) * P],
                                                 part[:, half, :], start=False, stop=False, skip_group_check=True)
                    last.then_inc(s_done, 1)

                def turn(n, s):
                    pe.wait_ge(hs_ready, 2 * n + 2)
                    for f in range(8):
                        last = pe.matmul(ps[:, 4, f * CAP:(f + 1) * CAP], hs[:, f // 4, (f % 4) * P:(f % 4 + 1) * P],
                                         ident2[:, :], start=True, stop=True)
                    last.then_inc(t_full, 1)
                    pe.wait_ge(pw_ready, n + 1)
                    for b in range(2):
                        last = pe.transpose(ps[:, 5, b * P:(b + 1) * P], pickw[:, s, b, :], ident[:, :])
                    last.then_inc(pt_full, 1)

                def second_product(n, s, place, gathered):
                    j = number(r, place)
                    pe.wait_ge(act_ready, n + 1)
                    if gathered is not None:
                        pe.wait_ge(x_hi, gathered)
                        pe.wait_ge(x_lo, gathered)
                    if not isinstance(n, int) or n > 0:
                        pe.wait_ge(y_lo, 2 * n)
                    pe.wait_ge(lo_done, 2 * j + 2)
                    wh, wl = wide(hi[place[1] % HLB]), wide(lo[place[1] % HLB])
                    for half in range(2):
                        col = slice(half * 512, (half + 1) * 512)
                        for k in range(4):
                            pe.matmul(ps[:, 6 + half, :], actp[:, s, k, :], wh[:, k, col], start=(k == 0), stop=False)
                            last = pe.matmul(ps[:, 6 + half, :], actp[:, s, k, :], wl[:, k, col], start=False,
                                             stop=(k == 3))
                        last.then_inc(y_full if half == 0 else chunk_done, 1)

                def expert(i, s, head=False, tail=False):
                    n = n0 + 2 * i + s
                    first_product(i, s, n)
                    more = s == 1 and not tail
                    if more:
                        if not head:
                            pe.wait_ge(y_lo, 2 * n - 2)
                        gather(i + 1)
                    if not head:
                        scatter(n - 2, s)
                    turn(n, s)
                    if not (head and s == 0):
                        second_product(n - 1, 1 - s, second_weights(i, s), 2 * (g0 + i) + 4 if more else None)

                if not isinstance(r, int):
                    pe.wait_ge(y_lo, 2 * n0)
                gather(0)
                for s in range(2):
                    expert(0, s, head=True)
                with pe.Fori(1, NE // 2 - 1) as i:
                    for s in range(2):
                        expert(i, s)
                for s in range(2):
                    expert(NE // 2 - 1, s, tail=True)
                scatter(n0 + NE - 2, 0)
                second_product(n0 + NE - 1, 1, (NE // 2 - 1, 5), None)
                scatter(n0 + NE - 1, 1)

            one_round(0)
            pe.wait_ge(routed, 1)
            rounds = pe.value_load(rounds_i[0:1, 0:1], min_val=1, max_val=4)
            with pe.If(rounds > 1):
                with pe.Fori(1, rounds) as r:
                    one_round(r)

        @block.scalar
        def _(act):
            pe_at = lambda step: act.wait_ge(pe_step, pe_count(step))
            dve_at = lambda step: act.wait_ge(dve_step, dve_count(step))
            steps_done = [0]
            ch = Chain(act, act_chain)

            def done(ins):
                ins.then_inc(act_step, 1)
                steps_done[0] += 1
                act.wait_ge(act_step, steps_done[0])

            act.wait_ge(made, 1)
            for t in range(4):
                act.wait_ge(in_landed["x" if t < 2 else "ctx"], 16)
                ch.link(act.activation(xnT[:, 0:2, :], xtok[:, t, :].rearrange("p (a n) -> p a n", a=2), ACT.Square,
                                       accum_out=stat[:, t:t + 1]))
            act.activation(stat[:, :], stat[:, :], ACT.Sqrt, scale=1.0 / D, bias=eps[:, 0:1]).then_inc(roots, 1)
            mixer_hi(act, 0)
            chunk = 0
            split = 1
            for step in STEPS:
                kind, j = step
                if kind in CHUNKED:
                    chunk += 1
                    if split < C0:
                        mixer_hi(act, split)
                        split += 1
                if kind == "TV":
                    dve_at(("TV", 0))
                    ch.link(act.activation(csilu[:, :], cols[:, 0:16], ACT.Silu))
                    act.wait_ge(in_landed["decay"], 16)
                    ch.link(act.activation(lgt[:, 0, :], lgd[:, :], ACT.Exp))
                    ch.link(act.activation(lgt[:, 1, :], lgt[:, 0, :], ACT.Copy, scale=-1.0, bias=1.0))
                    done(act.activation(lgt[:, 2, :], lgt[:, 1, :], ACT.Ln))
                elif kind == "XT":
                    pe_at(step)
                    for n, k in enumerate(((0, 1), (4,), (6,))[j]):
                        last = act.activation(xnT[:, k, :], ps[:, k % 6, :], ACT.Copy)
                    done(last)
                elif kind == "M":
                    if j == 6:
                        dve_at(("WO", 1))
                        for b in range(2):
                            ch.link(act.activation(hx2T[:, 0:4, :].rearrange("p a n -> p (a n)"), x1[:, b, :], ACT.Square,
                                                   accum_out=stat[:, b:b + 1]))
                        act.activation(stat[:, 0:2], stat[:, 0:2], ACT.Sqrt, scale=1.0 / D, bias=eps[:, 0:1])\
                           .then_inc(roots, 1)
                    pe_at(step)
                    done(act.activation(mrow[0:4, j % 2, :], ps[0:4, 6 if j < 4 or j >= 6 else 2, :], ACT.Copy))
                elif kind == "K":
                    if j == 0:
                        act.wait_ge(hx_mod, 1)
                        for k in range(KT):
                            last = act.activation(xnT[:, k, T:2 * T], xnT[:, k, T:2 * T], ACT.Identity,
                                                  scale=s1[:, k, 1:2], bias=modc[:, k, 1:2])
                        ch.link(last)
                        act.activation(hxh[:, :, :], xnT[:, :, 0:T], ACT.Copy).then_inc(hx_hi, 1)
                        act.activation(hch[:, :, :], xnT[:, :, T:2 * T], ACT.Copy).then_inc(hx_hi, 1)
                    pe_at(step)
                    done(act.activation(k_sb[:, :, T:2 * T], ps[:, 0:4, T:2 * T], ACT.Copy))
                elif kind == "V":
                    pe_at(step)
                    if j == 0:
                        dve_at(("Q", 0))
                    done(act.activation(v_sb[:, 0:2, :], ps[:, 0:2, :], ACT.Copy))
                elif kind == "S":
                    act.wait_ge(darg_ready, j + 1)
                    f, b = j, H + j
                    act.activation(att[:, 2:4, :], dist[:, :, :], ACT.Exp, scale=lgt[:, 0, f:f + 1], bias=lgt[:, 2, f:f + 1])
                    act.activation(g_sb[:, 0:2, :], dist[:, :, :], ACT.Exp, scale=lgt[:, 1, b:b + 1], bias=lgt[:, 2, b:b + 1])
                    done(act.activation(att[:, 0:2, :], darg[:, :, :], ACT.Exp))
                elif kind == "G":
                    pe_at(step)
                    dve_at(("S", j))
                    done(act.activation(g_sb[:, :, :], ps[:, 6:8, :].rearrange("p a (b t) -> p (a b) t", b=2), ACT.Silu))
                elif kind == "PV":
                    act.wait_ge(gvar_ready, j + 1)
                    done(act.activation(grs[:, :], gmv[:, :, 1], ACT.Sqrt, bias=eps[:, 1:2]))
                elif kind == "T":
                    act.wait_ge(prod_ready, j + 1)
                    done(act.activation(yth[:, :, :], g_sb[:, :, :], ACT.Copy))
                elif kind == "CH":
                    pe_at(step)
                    if j == 1:
                        dve_at(("CC", 0))
                    done(act.activation(ch_sb[:, :, :], ps[:, 0:2, :].rearrange("p a (b t) -> p (a b) t", b=2), ACT.Copy))
                elif kind == "CB":
                    act.wait_ge(prod_ready, H + j + 1)
                    done(act.activation(yth[:, :, :], conv_sb[:, :, :], ACT.Copy))
                elif kind in ("GA", "GB"):
                    pe_at(step)
                    dve_at({("GA", 0): ("CB", 1), ("GA", 1): ("GA", 0), ("GB", 0): ("GA", 1), ("GB", 1): ("GB", 0)}[step])
                    first = {("GA", 0): 2, ("GA", 1): 0, ("GB", 0): 2, ("GB", 1): 0}[step]
                    sig = act.activation(g_sb[:, :, :], ps[:, first:first + 2, :].rearrange("p a (b t) -> p (a b) t", b=2),
                                         ACT.Sigmoid)
                    if kind == "GA":
                        done(sig)
                    else:
                        sig.then_inc(gates_ready, 1)
                        act.wait_ge(prod_ready, H + 2 + j + 1)
                        done(act.activation(hch[:, 4 * j:4 * j + 4, :], racc[:, 4 * j:4 * j + 4, :], ACT.Copy))
                elif kind == "HT":
                    pe_at(step)
                    done(act.activation(hx2T[:, 0:4, :].rearrange("p (a b) t -> p a (b t)", b=2), ps[:, 0:2, :], ACT.Copy))
                elif kind == "LG":
                    act.wait_ge(logit_ready, 1)
                    done(act.activation(rt[:, :, 80:85], rt[:, :, 72:77], ACT.Exp))

            def one_round(r):
                n0, g0 = NE * r, (NE // 2) * r

                def gathered_hi(i):
                    for bank in range(2):
                        act.wait_ge(g_full, 2 * (g0 + i) + bank + 1)
                        act.activation(xg[:, :, 4 * bank:4 * bank + 4, 0:CAP].rearrange("p s k c -> p k s c"),
                                       ps[:, 6 + bank, :].rearrange("p (k s c) -> p k s c", k=4, s=2),
                                       ACT.Copy).then_inc(x_hi, 1)

                def rows_hi(n, s, w2_place):
                    act.wait_ge(cw_ready, n + 1)
                    if not isinstance(n, int) or n > 0:
                        act.wait_ge(s_done, n)
                    for half in range(2):
                        if half == 0:
                            act.wait_ge(y_full, n + 1)
                        else:
                            act.wait_ge(chunk_done, number(r, w2_place) - C0 + 1)
                        act.activation(yh[:, half, :], ps[:, 6 + half, :], ACT.Copy, scale=cw[:, s:s + 1])\
                           .then_inc(y_hi, 1)

                def expert(i, s, head=False, tail=False):
                    n = n0 + 2 * i + s
                    if not head:
                        rows_hi(n - 2, s, (i, 3 * s - 2))
                    if not (head and s == 0):
                        expert_hi(act, r, second_weights(i, s))
                    last_one = tail and s == 1
                    coming = first_half(i + s, 1 - s)
                    for half in range(2):
                        act.wait_ge(chunk_done, number(r, first_half(i, s)) - C0 + half + 1)
                        if half == 0 and (not isinstance(n, int) or n > 0):
                            act.wait_ge(t_full, n)
                            act.wait_ge(hs_ready, 2 * n)
                        act.activation(hs[:, half, :], ps[:, 4 + half, :], ACT.Copy).then_inc(hs_ready, 1)
                        if half == 0 and not last_one:
                            expert_hi(act, r, coming)
                    if s == 1 and not tail:
                        gathered_hi(i + 1)
                    act.wait_ge(t_full, n + 1)
                    if not isinstance(n, int) or n > 0:
                        act.wait_ge(act_ready, n)
                    act.activation(sa[:, :, :], ps[:, 4, 0:4 * CAP].rearrange("p (f c) -> p f c", f=4), ACT.Silu)\
                       .then_inc(sa_ready, 1)
                    act.wait_ge(pt_full, n + 1)
                    if not isinstance(n, int) or n > 1:
                        act.wait_ge(s_done, n - 1)
                    act.activation(sel[:, s, :], ps[:, 5, 0:T], ACT.Sign).then_inc(sel_ready, 1)
                    if not last_one:
                        expert_hi(act, r, nxt(coming))

                expert_hi(act, r, (0, 0))
                gathered_hi(0)
                expert_hi(act, r, (0, 1))
                for s in range(2):
                    expert(0, s, head=True)
                with act.Fori(1, NE // 2 - 1) as i:
                    for s in range(2):
                        expert(i, s)
                for s in range(2):
                    expert(NE // 2 - 1, s, tail=True)
                rows_hi(n0 + NE - 2, 0, second_weights(NE // 2 - 1, 1))
                expert_hi(act, r, (NE // 2 - 1, 5))
                rows_hi(n0 + NE - 1, 1, (NE // 2 - 1, 5))

            one_round(0)
            act.wait_ge(routed, 1)
            rounds = act.value_load(rounds_i[0:1, 0:1], min_val=1, max_val=4)
            with act.If(rounds > 1):
                with act.Fori(1, rounds) as r:
                    one_round(r)
            for b in range(2):
                act.wait_ge(squares, b + 1)
                act.activation(hs[:, :, :].rearrange("p a n -> p (a n)"), hx2[:, b, :], ACT.Square,
                               accum_out=stat[:, 2 + b:3 + b]).then_inc(act_chain, 1)
                ch.n += 1
                act.wait_ge(act_chain, ch.n)
                act.activation(stat[:, 2 + b:3 + b], stat[:, 2 + b:3 + b], ACT.Sqrt, scale=1.0 / D, bias=eps[:, 0:1])\
                   .then_inc(roots, 1)

        @block.vector
        def _(dve):
            pe_at = lambda step: dve.wait_ge(pe_step, pe_count(step))
            act_at = lambda step: dve.wait_ge(act_step, act_count(step))
            steps_done = [0]
            ch = Chain(dve, dve_chain)
            L = ch.link
            V = dve

            def done(ins):
                ins.then_inc(dve_step, 1)
                steps_done[0] += 1
                dve.wait_ge(dve_step, steps_done[0])

            def quad(first):
                return ps[:, first:first + 2, :].rearrange("p a (b t) -> p (a b) t", b=2)

            V.wait_ge(roots, 1)
            L(V.reciprocal(stat[:, :], stat[:, :]))
            for t in range(4):
                V.tensor_scalar(xtok[:, t, :], xtok[:, t, :], stat[:, t:t + 1], None, ALU.mult).then_inc(xn_ready, 1)
            V.wait_ge(xn_ready, 4)
            mixer_lo(dve, 0)
            split = 1
            for step in STEPS:
                kind, j = step
                if kind in CHUNKED and split < C0:
                    mixer_lo(dve, split)
                    split += 1
                if kind == "TV":
                    pe_at(step)
                    done(V.tensor_copy(cols[:, :], ps[:, 5, 0:64]))
                    act_at(("TV", 0))
                    cv = csilu[:, :].rearrange("p (v k) -> p k v", v=2)
                    L(V.tensor_copy(cs[:, :, 0:2], cv))
                    V.tensor_tensor(cs[:, :, 2:4], cv, cs[:, :, 0:2], ALU.subtract)
                    e, u, ln = lgt[:, 0, :], lgt[:, 1, :], lgt[:, 2, :]
                    L(V.tensor_scalar(lgt[:, 3, :], u, 1.0, None, ALU.subtract))
                    L(V.reciprocal(lgt[:, 3, :], lgt[:, 3, :]))
                    L(V.tensor_tensor(lgt[:, 3, :], lgt[:, 3, :], e, ALU.mult))
                    L(V.tensor_scalar(lgt[:, 3, :], lgt[:, 3, :], -1.0, None, ALU.mult))
                    L(V.tensor_tensor(lgt[:, 0, :], lgt[:, 3, :], ln, ALU.mult))
                    L(V.tensor_scalar(lgt[:, 1, :], lgt[:, 0, :], -1.0, None, ALU.mult))
                    L(V.tensor_scalar(lgt[:, 2, :], lgt[:, 0, :], float(T), None, ALU.mult))
                    continue
                if kind == "XT":
                    pe_at(step)
                    for k in ((2, 3), (5,), (7,))[j]:
                        last = V.tensor_copy(xnT[:, k, :], ps[:, k % 6, :])
                    done(last)
                elif kind == "MC":
                    pe_at(step)
                    done(V.tensor_copy(modc[:, 4 * j:4 * j + 4, :], ps[:, 7, 0:8].rearrange("p (f v) -> p f v", v=2)))
                elif kind == "MB":
                    pe_at(step)
                    src = ps[:, 7 if j >= 6 else 3, :]
                    col = slice(512 * (j % 2), 512 * (j % 2) + 512)
                    if j in (8, 9):
                        V.wait_ge(in_landed["norm2"], 16)
                        done(V.scalar_tensor_tensor(scale2[:, col], src, 1.0, norm2[:, col], ALU.add, ALU.mult))
                    else:
                        done(V.tensor_copy({2: gate1, 3: shift2, 5: gate2}[j // 2][:, col], src))
                elif kind == "K":
                    if j == 0:
                        for v in range(2):
                            last = V.scalar_tensor_tensor(s1[:, :, v], modc[:, 8:16, v], 1.0, cols[:, 16:24], ALU.add, ALU.mult)
                        L(last)
                        act_at(("XT", 2))
                        for k in range(KT):
                            last = V.tensor_scalar(xnT[:, k, 0:T], xnT[:, k, 0:T], s1[:, k, 0:1], modc[:, k, 0:1],
                                                   ALU.mult, ALU.add)
                        last.then_inc(hx_mod, 1)
                        V.wait_ge(hx_mod, 1)
                        V.wait_ge(hx_hi, 1)
                        V.tensor_tensor(hxl[:, :, :], xnT[:, :, 0:T], hxh[:, :, :], ALU.subtract).then_inc(hx_lo, 1)
                        V.wait_ge(hx_hi, 2)
                        V.tensor_tensor(hcl[:, :, :], xnT[:, :, T:2 * T], hch[:, :, :], ALU.subtract).then_inc(hx_lo, 1)
                if kind in ("K", "Q"):
                    pe_at(step)
                    if kind == "K":
                        act_at(step)
                        src, dst, tmp = ps[:, 0:4, 0:T], k_sb[:, :, 0:T], q_sb
                        half = lambda lo_p, hi_p: ps[lo_p:hi_p, 0:4, 0:T]
                    else:
                        src, dst, tmp = quad(4), q_sb[:, :, :], att
                        half = lambda lo_p, hi_p: ps[lo_p:hi_p, 4:6, :].rearrange("p a (b t) -> p (a b) t", b=2)
                    two = lambda a: a.rearrange("p (h a) t -> p h a t", a=2)
                    for hh in range(2):
                        t2 = slice(2 * hh, 2 * hh + 2)
                        V.tensor_tensor(dst[:, t2, :], src[:, t2, :], rope[:, 0, :, :], ALU.mult)
                        V.tensor_tensor(tmp[0:64, t2, :], half(64, 128)[:, t2, :], rope[64:128, 1, :, :], ALU.mult)
                        last = V.tensor_tensor(tmp[64:128, t2, :], half(0, 64)[:, t2, :], rope[0:64, 1, :, :], ALU.mult)
                    L(last)
                    done(V.tensor_tensor(dst, dst, tmp[:, :, :], ALU.add))
                elif kind == "V":
                    pe_at(step)
                    if j > 0:
                        pe_at(("PV", j - 1))
                    done(V.tensor_copy(v_sb[:, 2:4, :], ps[:, 2:4, :]))
                elif kind == "S":
                    if j > 0:
                        pe_at(("T", j - 1))
                    lf, nlb = lgt[:, 0, j:j + 1], lgt[:, 1, H + j:H + j + 1]
                    V.tensor_scalar(darg[:, :, :], dist[:, :, :], 0.0, lf, ALU.max, ALU.mult)
                    L(V.tensor_scalar(att[:, 0:2, :], dist[:, :, :], 0.0, nlb, ALU.min, ALU.mult))
                    V.tensor_tensor(darg[:, :, :], darg[:, :, :], att[:, 0:2, :], ALU.add).then_inc(darg_ready, 1)
                    act_at(step)
                    L(V.tensor_tensor(att[:, 2:4, :], att[:, 2:4, :], g_sb[:, 0:2, :], ALU.add))
                    pe_at(step)
                    done(V.scalar_tensor_tensor(att[:, :, :], quad(4), QK ** -0.5, att[:, :, :], ALU.mult, ALU.mult))
                elif kind == "PV":
                    pe_at(step)
                    for b in range(2):
                        last = V.bn_stats(gst[:, b, :], ps[:, 4 + b, :])
                    L(last)
                    for b in range(2):
                        last = V.bn_aggr(gmv[:, b, :], gst[:, b, :])
                    last.then_inc(gvar_ready, 1)
                    act_at(step)
                    L(V.reciprocal(grs[:, :], grs[:, :]))
                    for b in range(2):
                        last = V.tensor_scalar(yn[:, b, :], ps[:, 4 + b, :], gmv[:, b, 0:1], grs[:, b:b + 1],
                                               ALU.subtract, ALU.mult)
                    done(last)
                elif kind == "T":
                    pe_at(step)
                    act_at(("G", j))
                    for e in range(4):
                        n = 24 + 4 * j + e
                        last = V.scalar_tensor_tensor(g_sb[:, e, :], ps[:, 6 + e // 2, T * (e % 2):T * (e % 2 + 1)],
                                                      cols[:, n:n + 1], g_sb[:, e, :], ALU.mult, ALU.mult)
                    last.then_inc(prod_ready, 1)
                    act_at(step)
                    done(V.tensor_tensor(ytl[:, :, :], g_sb[:, :, :], yth[:, :, :], ALU.subtract))
                elif kind in ("RO", "CO"):
                    pe_at(step)
                    acc = (racc if kind == "RO" else cacc)[:, :, :].rearrange("p (a b) t -> p a (b t)", b=2)
                    if j == 0:
                        done(V.tensor_copy(acc, ps[:, 4:8, :]))
                    else:
                        done(V.tensor_tensor(acc, acc, ps[:, 4:8, :], ALU.add))
                elif kind == "CC":
                    pe_at(step)
                    act_at(("CH", j))
                    L(V.tensor_tensor(u_sb[:, :, :], quad(2), ch_sb[:, :, :], ALU.mult))
                    grid = lambda t, f: t[:, f, :].rearrange("p (r c) -> p r c", c=GRID)
                    tap = lambda n, f: cols[:, 40 + 8 * n + 4 * j + f:41 + 8 * n + 4 * j + f]
                    for f in range(4):
                        last = V.tensor_scalar(conv_sb[:, f, :], u_sb[:, f, :], tap(1, f), None, ALU.mult)
                    L(last)
                    for n, to, frm in ((0, slice(1, GRID), slice(0, GRID - 1)), (2, slice(0, GRID - 1), slice(1, GRID))):
                        for f in range(4):
                            last = V.scalar_tensor_tensor(grid(conv_sb, f)[:, :, to], grid(u_sb, f)[:, :, frm], tap(n, f),
                                                          grid(conv_sb, f)[:, :, to], ALU.mult, ALU.add)
                        if n == 0:
                            L(last)
                    done(last)
                elif kind == "CB":
                    pe_at(step)
                    V.tensor_tensor(conv_sb[:, :, :], quad(0), conv_sb[:, :, :], ALU.mult).then_inc(prod_ready, 1)
                    act_at(step)
                    V.wait_ge(prod_ready, H + j + 1)
                    done(V.tensor_tensor(ytl[:, :, :], conv_sb[:, :, :], yth[:, :, :], ALU.subtract))
                elif kind == "GA":
                    act_at(step)
                    part = racc[:, 4 * j:4 * j + 4, :]
                    done(V.tensor_tensor(part, part, g_sb[:, :, :], ALU.mult))
                elif kind == "GB":
                    V.wait_ge(gates_ready, j + 1)
                    ra, ca = racc[:, 4 * j:4 * j + 4, :], cacc[:, 4 * j:4 * j + 4, :]
                    L(V.tensor_tensor(ca, ca, g_sb[:, :, :], ALU.mult))
                    V.tensor_tensor(ra, ra, ca, ALU.add).then_inc(prod_ready, 1)
                    act_at(step)
                    V.wait_ge(prod_ready, H + 2 + j + 1)
                    done(V.tensor_tensor(hcl[:, 4 * j:4 * j + 4, :], ra, hch[:, 4 * j:4 * j + 4, :], ALU.subtract))
                elif kind == "WO":
                    pe_at(step)
                    V.wait_ge(in_landed["xres"], 16)
                    col = slice(512 * j, 512 * j + 512)
                    for b in range(2):
                        last = V.tensor_tensor(x1[:, b, col], ps[:, 4 + 2 * j + b, :], gate1[:, col], ALU.mult)
                    L(last)
                    done(V.tensor_tensor(x1[:, :, col], x1[:, :, col], xres[:, :, col], ALU.add))
                elif kind == "HT":
                    V.wait_ge(roots, 2)
                    L(V.reciprocal(stat[:, 0:2], stat[:, 0:2]))
                    for b in range(2):
                        last = V.scalar_tensor_tensor(hx2[:, b, :], x1[:, b, :], stat[:, b:b + 1], scale2[:, :], ALU.mult, ALU.mult)
                    L(last)
                    V.tensor_tensor(hx2[:, :, :], hx2[:, :, :], shift2[:, :].unsqueeze(1).to_broadcast([P, 2, D]),
                                    ALU.add).then_inc(hx2_ready, 1)
                    pe_at(step)
                    done(V.tensor_copy(hx2T[:, 4:8, :].rearrange("p (a b) t -> p a (b t)", b=2), ps[:, 2:4, :]))
                elif kind == "LG":
                    pe_at(step)
                    V.wait_ge(in_landed["router"], 96)
                    R = lambda a, b: rt[:, :, a:b]
                    B = lambda t, n: t.to_broadcast([P, 2, n])
                    first_of = desc[:, :].unsqueeze(1).to_broadcast([P, 2, 8])
                    L(V.tensor_tensor(lg[:, :, :], ps[:, 4, 0:128].rearrange("p (b n) -> p b n", b=2)[:, :, 0:NG + NE],
                                      rbias[:, :].unsqueeze(1).to_broadcast([P, 2, NG + NE]), ALU.add))

                    def top(values, n, m, key, at_key):
                        L(V.reduce_max(m, values, AX.X))
                        L(V.tensor_tensor(key, values, B(m, n), ALU.is_equal))
                        L(V.tensor_tensor(key, key, first_of[:, :, 0:n], ALU.mult))
                        L(V.reduce_max(at_key, key, AX.X))
                        L(V.tensor_tensor(key, key, B(at_key, n), ALU.is_equal))

                    Lg = lg[:, :, 0:NG]
                    Le = lg[:, :, NG:].rearrange("p b (g e) -> p b g e", g=NG)
                    top(Lg, NG, R(0, 1), R(4, 8), R(1, 2))
                    group = R(4, 8).unsqueeze(3).to_broadcast([P, 2, NG, EPG])
                    L(V.tensor_tensor(R(16, 48).rearrange("p b (g e) -> p b g e", g=NG), Le, group, ALU.mult))
                    L(V.reduce_sum(R(8, 16), R(16, 48).rearrange("p b (g e) -> p b e g", g=NG), AX.X))
                    top(R(8, 16), EPG, R(2, 3), R(48, 56), R(1, 2))
                    L(V.scalar_tensor_tensor(R(56, 64), R(48, 56), -BIG, R(8, 16), ALU.mult, ALU.add))
                    top(R(56, 64), EPG, R(3, 4), R(64, 72), R(1, 2))
                    V.tensor_tensor(R(72, 76), Lg, B(R(0, 1), NG), ALU.subtract)
                    V.tensor_tensor(R(76, 77), R(3, 4), R(2, 3), ALU.subtract).then_inc(logit_ready, 1)
                    act_at(step)
                    L(V.reduce_sum(R(85, 86), R(80, 84), AX.X))
                    L(V.tensor_scalar(R(86, 87), R(84, 85), 1.0, None, ALU.add))
                    L(V.tensor_tensor(R(86, 87), R(86, 87), R(85, 86), ALU.mult))
                    L(V.reciprocal(R(87, 88), R(86, 87)))
                    L(V.tensor_tensor(R(88, 89), R(87, 88), R(84, 85), ALU.mult))
                    L(V.tensor_tensor(R(8, 16), R(48, 56), B(R(87, 88), 8), ALU.mult))
                    L(V.tensor_tensor(R(56, 64), R(64, 72), B(R(88, 89), 8), ALU.mult))
                    L(V.tensor_tensor(R(8, 16), R(8, 16), R(56, 64), ALU.add))
                    L(V.tensor_tensor(R(48, 56), R(48, 56), R(64, 72), ALU.add))
                    for src, dst in ((R(8, 16), combx[:, :, 0:NE]), (R(48, 56), mask[:, :, :])):
                        last = V.tensor_tensor(dst.rearrange("p b (g e) -> p b g e", g=NG),
                                               src.unsqueeze(2).to_broadcast([P, 2, NG, EPG]), group, ALU.mult)
                    done(last)
                elif kind == "PS":
                    pe_at(step)
                    L(V.scalar_tensor_tensor(posx[:, :, 0:NE], ps[:, 5, 0:2 * NE].rearrange("p (b e) -> p b e", b=2), 1.0,
                                             mask[:, :, :], ALU.add, ALU.mult))
                    L(V.tensor_scalar(posx[:, :, 0:NE], posx[:, :, 0:NE], 1.0, None, ALU.subtract))
                    for q in range(1, 4):
                        V.tensor_scalar(posx[:, :, q * NE:(q + 1) * NE], posx[:, :, 0:NE], float(CAP * q), None, ALU.subtract)
                        V.tensor_copy(combx[:, :, q * NE:(q + 1) * NE], combx[:, :, 0:NE])
                    L(V.reduce_max(rmax[:, 0:1], ps[:, 5, 2 * NE:3 * NE], AX.X))
                    L(V.tensor_scalar(rmax[:, 1:2], rmax[:, 0:1], float(CAP), 1.0, ALU.is_gt, ALU.add))
                    for q in (2, 3):
                        L(V.scalar_tensor_tensor(rmax[:, 1:2], rmax[:, 0:1], float(CAP * q), rmax[:, 1:2], ALU.is_gt, ALU.add))
                    L(V.tensor_copy(rounds_i[0:1, 0:1], rmax[0:1, 1:2]))
                    V.nop().then_inc(routed, 1)
                    done(V.nop())

            def one_round(r):
                n0, g0 = NE * r, (NE // 2) * r

                def pick_pair(i):
                    if not isinstance(r, int) or not isinstance(i, int) or i > 0:
                        V.wait_ge(g_full, 2 * (g0 + i))
                    for s in range(2):
                        for b in range(2):
                            last = V.tensor_scalar(pick[:, b, CAP * s:CAP * (s + 1)], slot_no[:, 0:CAP],
                                                   posx[:, b, bass.ds(n0 + 2 * i + s, 1)], None, ALU.is_equal)
                    last.then_inc(p_ready, 1)

                def weigh(i, s):
                    n = n0 + 2 * i + s
                    if not isinstance(n, int) or n >= 2:
                        V.wait_ge(pt_full, n - 1)
                    for b in range(2):
                        last = V.tensor_scalar(pickw[:, s, b, :], slot_no[:, :], posx[:, b, bass.ds(n, 1)],
                                               combx[:, b, bass.ds(n, 1)], ALU.is_equal, ALU.mult)
                    last.then_inc(pw_ready, 1)

                def gathered_lo(i):
                    for bank in range(2):
                        V.wait_ge(x_hi, 2 * (g0 + i) + bank + 1)
                        k = slice(4 * bank, 4 * bank + 4)
                        V.tensor_tensor(xg[:, :, k, CAP:P].rearrange("p s k c -> p k s c"),
                                        ps[:, 6 + bank, :].rearrange("p (k s c) -> p k s c", k=4, s=2),
                                        xg[:, :, k, 0:CAP].rearrange("p s k c -> p k s c"), ALU.subtract).then_inc(x_lo, 1)

                def rows_lo(n, s):
                    for half in range(2):
                        V.wait_ge(y_hi, 2 * n + half + 1)
                        V.scalar_tensor_tensor(yl[:, half, :], ps[:, 6 + half, :], cw[:, s:s + 1], yh[:, half, :],
                                               ALU.mult, ALU.subtract).then_inc(y_lo, 1)

                def expert(i, s, head=False, tail=False):
                    n = n0 + 2 * i + s
                    if not head:
                        rows_lo(n - 2, s)
                    if not (head and s == 0):
                        expert_lo(dve, r, second_weights(i, s))
                    last_one = tail and s == 1
                    coming = first_half(i + s, 1 - s)
                    if not last_one:
                        expert_lo(dve, r, coming)
                    if s == 1 and not tail:
                        gathered_lo(i + 1)
                    if s == 0 and not tail:
                        pick_pair(i + 1)
                    V.wait_ge(sa_ready, n + 1)
                    if not isinstance(n, int) or n > 1:
                        V.wait_ge(y_lo, 2 * n - 2)
                    if not isinstance(n, int) or n > 0:
                        V.wait_ge(act_ready, n)
                    up = ps[:, 4, 4 * CAP:8 * CAP].rearrange("p (f c) -> p f c", f=4)
                    V.tensor_tensor(actp[:, s, :, 0:CAP], up, sa[:, :, :], ALU.mult)
                    V.tensor_tensor(am[:, :, :], up, sa[:, :, :], ALU.mult).then_inc(am_ready, 1)
                    V.wait_ge(am_ready, n + 1)
                    V.tensor_tensor(actp[:, s, :, CAP:P], am[:, :, :], actp[:, s, :, 0:CAP], ALU.subtract).then_inc(act_ready, 1)
                    V.wait_ge(sel_ready, n + 1)
                    V.reduce_sum(cw[:, s:s + 1], ps[:, 5, 0:T], AX.X).then_inc(cw_ready, 1)
                    if not last_one:
                        weigh(i + s, 1 - s)
                    if not last_one:
                        expert_lo(dve, r, nxt(coming))

                pick_pair(0)
                weigh(0, 0)
                expert_lo(dve, r, (0, 0))
                gathered_lo(0)
                expert_lo(dve, r, (0, 1))
                for s in range(2):
                    expert(0, s, head=True)
                with dve.Fori(1, NE // 2 - 1) as i:
                    for s in range(2):
                        expert(i, s)
                for s in range(2):
                    expert(NE // 2 - 1, s, tail=True)
                rows_lo(n0 + NE - 2, 0)
                expert_lo(dve, r, (NE // 2 - 1, 5))
                rows_lo(n0 + NE - 1, 1)
                V.wait_ge(s_done, n0 + NE)

            one_round(0)
            dve.wait_ge(routed, 1)
            rounds = dve.value_load(rounds_i[0:1, 0:1], min_val=1, max_val=4)
            with dve.If(rounds > 1):
                with dve.Fori(1, rounds) as r:
                    one_round(r)
            dve.wait_ge(in_landed["finw"], 16)
            for b in range(2):
                L(V.tensor_tensor(hx2[:, b, :], ps[:, 2 * b:2 * b + 2, :].rearrange("p a n -> p (a n)"), gate2[:, :], ALU.mult))
                V.tensor_tensor(hx2[:, b, :], hx2[:, b, :], x1[:, b, :], ALU.add).then_inc(squares, 1)
            for b in range(2):
                V.wait_ge(roots, 3 + b)
                L(V.reciprocal(stat[:, 2 + b:3 + b], stat[:, 2 + b:3 + b]))
                V.scalar_tensor_tensor(hx2[:, b, :], hx2[:, b, :], stat[:, 2 + b:3 + b], finw[:, :], ALU.mult,
                                       ALU.mult).then_inc(fin_ready, 1)


CONSTS = [("ident", P), ("rope", 4 * T), ("dist", 2 * T), ("slot_no", P), ("ident2", CAP), ("desc", 8),
          ("tri", P), ("ones", P), ("selc", 2)]
CONST_AT = {}
for _name, _n in CONSTS:
    CONST_AT[_name] = sum(n for m, n in CONSTS[:len(CONST_AT)])
CONST_W = sum(n for _, n in CONSTS)


def constant_table():
    t = np.zeros((P, CONST_W), np.float32)

    def put(name, a):
        a = np.asarray(a, np.float32)
        a = a.reshape(a.shape[0], -1)
        t[:a.shape[0], CONST_AT[name]:CONST_AT[name] + a.shape[1]] = a

    p = np.arange(P)
    put("ident", np.eye(P))
    nf = QK // 4
    inv = np.float32(10000.0) ** (-np.arange(nf, dtype=np.float32) / np.float32(nf))
    tok = np.arange(T)
    ang = np.stack([(tok // GRID).astype(np.float32)[None, :] * inv[p % nf][:, None],
                    (tok % GRID).astype(np.float32)[None, :] * inv[p % nf][:, None]], 1).astype(np.float32)
    sign = np.where(p < nf, 1.0, -1.0)[:, None, None]
    put("rope", np.stack([np.cos(ang), np.sin(ang) * sign], 1))
    put("dist", tok[None, None, :] - (P * np.arange(2)[None, :, None] + p[:, None, None]))
    put("slot_no", np.broadcast_to(p[None, :] % CAP, (P, P)))
    put("ident2", np.concatenate([np.eye(CAP)] * 2))
    put("desc", np.broadcast_to(np.arange(8, 0, -1), (P, 8)))
    put("tri", p[:, None] < p[None, :])
    put("ones", np.ones((P, P)))
    put("selc", [[1, 0], [0, 1], [1, 0], [0, 1], [1, 1]])
    return t


_INS = ["x", "c", "ctx", "c_ctx", "w_mod", "b_mod", "norm1_w", "norm2_w", "w_in", "ret_log_decay", "ret_gn_w",
        "w_ret_o", "conv_w", "w_conv_o", "w_out", "router_group_w", "router_group_b", "router_expert_w",
        "router_expert_b", "expert_w13", "expert_w2", "final_norm_w"]


def kernel(**inputs):
    import concourse.bacc as bacc
    from concourse.bass_utils import run_bass_kernel_spmd

    nc = bacc.Bacc("TRN2", target_bir_lowering=False, num_devices=1)
    arrays, args = {}, []
    for name in _INS + ["consts"]:
        a = constant_table() if name == "consts" else np.ascontiguousarray(inputs[name])
        arrays[f"in_{name}"] = a
        args.append(nc.dram_tensor(f"in_{name}", a.shape, mybir.dt.from_np(a.dtype), kind="ExternalInput").ap())
    out = nc.dram_tensor("out_0", (1, T, D), F32, kind="ExternalOutput").ap()
    block_kernel(nc, *args, out)
    r = run_bass_kernel_spmd(nc, [arrays], core_ids=[0])
    return r.results[0]["out_0"]
```

```python
from contextlib import ExitStack

import numpy as np

import concourse.bass as bass
from concourse import mybir

F32 = mybir.dt.float32
F32R = mybir.dt.float32r
I32 = mybir.dt.int32
ACT = mybir.ActivationFunctionType
ALU = mybir.AluOpType
AX = mybir.AxisListType

P = 128
D = 1024
T = 256
GRID = 64
H = 4
QK = 256
DV = 512
KT = D // P
NE = 32
NG = 4
EPG = 8
HID = 512
CAP = 64
NORM_EPS = 1e-6
GN_EPS = 1e-5
BIG = 3.0e38

W_Q, W_K, W_V, W_G, W_CB, W_CC, W_CH, W_GATE = 0, 2, 4, 8, 12, 14, 16, 18

RAW = 3
AHEAD = 3
HL = 2
HLB = 3

STEPS = ([("TV", 0), ("XT", 0), ("XT", 1), ("XT", 2)]
         + [(k, j) for j in range(4) for k in ("M", "MC")]
         + [("Q", 0), ("K", 0), ("M", 4), ("V", 0), ("S", 0), ("G", 0), ("PV", 0), ("V", 1), ("T", 0), ("M", 5), ("RO", 0),
            ("M", 6), ("S", 1), ("G", 1), ("PV", 1), ("K", 1), ("T", 1), ("M", 7), ("RO", 1),
            ("M", 8), ("Q", 1), ("V", 2), ("S", 2), ("G", 2), ("PV", 2), ("V", 3), ("T", 2), ("M", 9), ("RO", 2),
            ("M", 10), ("S", 3), ("G", 3), ("PV", 3), ("CH", 0), ("T", 3), ("M", 11), ("RO", 3),
            ("CC", 0), ("CB", 0), ("CH", 1), ("CC", 1), ("CO", 0), ("CB", 1), ("GA", 0), ("CO", 1),
            ("GA", 1), ("GB", 0), ("GB", 1), ("MB", 4), ("MB", 5), ("WO", 0), ("WO", 1),
            ("MA", 6), ("MA", 7), ("MB", 8), ("MB", 9), ("HT", 0), ("MA", 10), ("MA", 11), ("LG", 0), ("PS", 0)])
M_BANK = {5: 4, 6: 0, 7: 4, 8: 0, 9: 4, 10: 0, 11: 4}
CHUNKED = ("M", "K", "Q", "V", "G", "RO", "CH", "CC", "CB", "CO", "GA", "GB", "WO")
CHUNKS = [s for s in STEPS if s[0] in CHUNKED]
C0 = len(CHUNKS)
assert C0 % RAW == 0

ACT_KINDS = ("XT", "M", "K", "V", "S", "G", "PV", "T", "CH", "CB", "GA", "GB", "MA", "HT", "LG")
DVE_KINDS = ("TV", "XT", "MC", "MB", "K", "Q", "V", "S", "PV", "T", "RO", "CC", "CB", "CO", "GA", "GB",
             "WO", "HT", "LG", "PS")


def pe_count(step):
    return sum(s[0] not in CHUNKED for s in STEPS[:STEPS.index(step) + 1])


def act_count(step):
    return sum(s[0] in ACT_KINDS for s in STEPS[:STEPS.index(step) + 1])


DVE_STEPS = list(STEPS)
DVE_STEPS.remove(("K", 1))
DVE_STEPS.insert(DVE_STEPS.index(("T", 1)) + 1, ("K", 1))


def dve_count(step):
    return sum(s[0] in DVE_KINDS for s in DVE_STEPS[:DVE_STEPS.index(step) + 1])


def block_kernel(nc, x, c, ctx_in, c_ctx, w_mod, b_mod, norm1_w, norm2_w, w_in, ret_log_decay, ret_gn_w,
                 w_ret_o, conv_w, w_conv_o, w_out, router_group_w, router_group_b, router_expert_w,
                 router_expert_b, expert_w13, expert_w2, final_norm_w, consts, out):
    stack = ExitStack()
    with stack:
        def sem(name):
            return stack.enter_context(nc.semaphore(name))

        BASE = -(-nc.sbuf_base // 64) * 64

        def at(name, kib, shape, dt=F32):
            return nc.alloc_sbuf_tensor_at(name, shape, dt, offset=BASE + int(kib * 1024))

        raw = [at(f"raw{i}", 16 * i, [P, 8, 512]) for i in range(RAW)]
        hi = [at(f"hi{i}", 48 + 16 * i, [P, 8, 512], F32R) for i in range(HL)] + [at("hi2", 128, [P, 8, 512], F32R)]
        lo = [at(f"lo{i}", 80 + 16 * i, [P, 8, 512], F32R) for i in range(HL)] + [at("lo2", 144, [P, 8, 512], F32R)]
        hxh = at("hxh", 112, [P, KT, T], F32R)
        hxl = at("hxl", 120, [P, KT, T], F32R)
        hch = at("hch", 128, [P, KT, T], F32R)
        hcl = at("hcl", 136, [P, KT, T], F32R)
        xtok = at("xtok", 128, [P, 4, D])
        xnT = at("xnT", 144, [P, KT, 2 * T])
        v_sb = at("v_sb", 144, [P, 4, DV])
        racc = at("racc", 152, [P, KT, T])
        cacc = at("cacc", 144, [P, KT, T])
        k_sb = at("k_sb", 160, [P, 4, 2 * T])
        u_sb = at("u_sb", 160, [P, 4, T])
        conv_sb = at("conv_sb", 164, [P, 4, T])
        q_sb = at("q_sb", 168, [P, 4, T])
        ch_sb = at("ch_sb", 168, [P, 4, T])
        att = at("att", 172, [P, 4, T])
        yn = at("yn", 172, [P, 2, DV])
        g_sb = at("g_sb", 176, [P, 4, T])
        yth = at("yth", 180, [P, 4, T], F32R)
        ytl = at("ytl", 184, [P, 4, T], F32R)
        rope = at("rope", 188, [P, 2, 2, T])
        dist = at("dist", 192, [P, 2, T])
        mrow = at("mrow", 194, [5, 2, 512])
        mstack = at("mstack", 196, [40, 512])
        gate1 = at("gate1", 188, [P, D])
        darg = at("darg", 202, [P, 2, T])
        zrow = at("zrow", 202, [1, 512])
        x1 = at("x1", 112, [P, 2, D])
        xres = at("xres", 120, [P, 2, D])
        hx2 = at("hx2", 120, [P, 2, D])
        hx2T = at("hx2T", 160, [P, KT, T])
        shift2 = at("shift2", 168, [P, D])
        scale2 = at("scale2", 176, [P, D])
        norm2 = at("norm2", 180, [P, D])
        xg = at("xg", 160, [P, 2, KT, P], F32R)
        hs = at("hs", 168, [P, 2, HID])
        actp = at("actp", 172, [P, 2, 4, P], F32R)
        yh = at("yh", 176, [P, 2, 512], F32R)
        yl = at("yl", 180, [P, 2, 512], F32R)
        pick = at("pick", 184, [P, 2, P])
        pickw = at("pickw", 185, [P, 2, 2, P])
        am = at("am", 187, [P, 4, CAP])
        sel = at("sel", 188, [P, 2, T], F32R)
        sa = at("sa", 190, [P, 4, CAP])
        posx = at("posx", 191, [P, 2, 4 * NE])
        combx = at("combx", 192, [P, 2, 4 * NE])
        wsum = at("wsum", 193, [P, T])
        finw = at("finw", 194, [P, D])
        gate2 = at("gate2", 198, [P, D])
        small_at = [204.0]

        def small(name, shape, dt=F32):
            n = 1
            for s in shape[1:]:
                n *= s
            t = at(name, small_at[0], shape, dt)
            small_at[0] += -(-n * 4 // 32) * 32 / 1024
            return t

        ident = small("ident", [P, P])
        tri = at("tri", 193, [P, P])
        ones = at("ones", 193.5, [P, P])
        slot_no = small("slot_no", [P, P])
        vrow = at("vrow", 202, [64, P])
        cols = small("cols", [P, 64])
        csilu = small("csilu", [P, 16])
        cs = small("cs", [P, 8, 4], F32R)
        selc = small("selc", [5, 2])
        selm = small("selm", [40, 8])
        modc = small("modc", [P, 16, 2])
        s1 = small("s1", [P, 8, 2])
        lgd = small("lgd", [P, 8])
        lgt = small("lgt", [P, 4, 8])
        stat = small("stat", [P, 4])
        gst = small("gst", [P, 2, 6])
        gmv = small("gmv", [P, 2, 2])
        grs = small("grs", [P, 2])
        cw = small("cw", [P, 2])
        ident2 = small("ident2", [P, CAP])
        desc = small("desc", [P, 8])
        eps = small("eps", [P, 2])
        loaded = small("loaded", [P, 2])
        rmax = small("rmax", [P, 2])
        rounds_i = small("rounds_i", [1, 1], I32)
        rw = at("rw", 172, [P, KT, NG + NE])
        rbias = at("rbias", 174, [P, NG + NE])
        lg = at("lg", 174.25, [P, 2, NG + NE])
        rt = at("rt", 174.75, [P, 2, 96])
        mask = at("mask", 175.5, [P, 2, NE])

        ps = stack.enter_context(nc.psum_tensor("ps", [P, 8, 512], F32))

        landed = [sem(f"landed{i}") for i in range(RAW)]
        hi_done, lo_done, half_used, chunk_done = sem("hi_done"), sem("lo_done"), sem("half_used"), sem("chunk_done")
        pe_step, act_step, dve_step = sem("pe_step"), sem("act_step"), sem("dve_step")
        act_chain, dve_chain = sem("act_chain"), sem("dve_chain")
        in_landed = {n: sem(f"in_{n}") for n in ("consts", "vecs", "x", "ctx", "decay", "xres", "norm2", "router", "finw")}
        brow_landed = [sem(f"brow{i}") for i in range(2)]
        stacked, biases_landed = sem("stacked"), sem("biases_landed")
        made = sem("constants_made")
        xn_ready, hx_mod, hx_hi, hx_lo = sem("xn_ready"), sem("hx_mod"), sem("hx_hi"), sem("hx_lo")
        squares, roots = sem("squares"), sem("roots")
        silu_ready, silu_parts, log_ready = sem("silu_ready"), sem("silu_parts"), sem("log_ready")
        darg_ready, decay_ready = sem("darg_ready"), sem("decay_ready")
        gvar_ready, groot_ready = sem("gvar_ready"), sem("groot_ready")
        prod_ready, prod_hi = sem("prod_ready"), sem("prod_hi")
        gates_ready, hx2_ready, logit_ready, exp_ready = (
            sem(n) for n in ("gates_ready", "hx2_ready", "logit_ready", "exp_ready"))
        am_ready = sem("am_ready")
        routed, out_done = sem("routed"), sem("out_done")
        p_ready, pw_ready, g_full, x_hi, x_lo = (sem(n) for n in ("p_ready", "pw_ready", "g_full", "x_hi", "x_lo"))
        hs_ready, t_full, sa_ready, act_ready = (
            sem(n) for n in ("hs_ready", "t_full", "sa_ready", "act_ready"))
        pt_full, sel_ready, cw_ready, y_full, y_hi, y_lo, s_done = (
            sem(n) for n in ("pt_full", "sel_ready", "cw_ready", "y_full", "y_hi", "y_lo", "s_done"))
        fin_ready = sem("fin_ready")

        def k_rows(w):
            return w.rearrange("(k p) n -> p k n", p=P)

        w_in_v = k_rows(w_in[0])
        w_mod_v = k_rows(w_mod[0])
        w_out_v = k_rows(w_out[0])
        w_ro_v = w_ret_o[0].rearrange("(h k p) n -> h p k n", k=4, p=P)
        w_co_v = w_conv_o[0].rearrange("(h k p) n -> h p k n", k=4, p=P)
        w13_v = expert_w13[0].rearrange("e (k p) n -> e p k n", p=P)
        w2_v = expert_w2[0].rearrange("e (k p) n -> e p k n", p=P)

        def wide(t):
            return t[:, :, :].rearrange("p (k a) n -> p k (a n)", a=2)

        def col512(v, j):
            return v[:, :, 512 * j:512 * (j + 1)]

        def chunk_source(kind, j):
            at_col = {"K": W_K, "Q": W_Q, "V": W_V, "G": W_G, "CB": W_CB, "CC": W_CC, "CH": W_CH,
                      "GA": W_GATE, "GB": W_GATE + 2}
            if kind == "M":
                return False, col512(w_mod_v, j)
            if kind == "WO":
                return False, col512(w_out_v, j)
            if kind == "RO":
                return True, w_ro_v[j]
            if kind == "CO":
                return True, w_co_v[j]
            return False, col512(w_in_v, at_col[kind] + j)

        class Chain:
            def __init__(self, eng, s):
                self.eng, self.s, self.n = eng, s, 0

            def link(self, ins):
                self.n += 1
                ins.then_inc(self.s, 1)
                self.eng.wait_ge(self.s, self.n)

        def wait_pe(eng, step):
            if step[0] in CHUNKED:
                eng.wait_ge(half_used, 2 * CHUNKS.index(step) + 2)
            else:
                eng.wait_ge(pe_step, pe_count(step))

        def split_hi(eng, raw_slot, lands, part_slot, halves=(0, 1)):
            eng.wait_ge(landed[raw_slot], lands)
            for half in halves:
                k = slice(4 * half, 4 * half + 4)
                eng.activation(hi[part_slot][:, k, :], raw[raw_slot][:, k, :], ACT.Copy).then_inc(hi_done, 1)

        def split_lo(eng, j, raw_slot, part_slot, halves=(0, 1)):
            for half in halves:
                k = slice(4 * half, 4 * half + 4)
                eng.wait_ge(hi_done, 2 * j + half + 1)
                eng.tensor_tensor(lo[part_slot][:, k, :], raw[raw_slot][:, k, :], hi[part_slot][:, k, :],
                                  ALU.subtract).then_inc(lo_done, 1)

        class MixerSplits:
            def __init__(self, eng, is_hi):
                self.eng, self.is_hi, self.half, self.chunk = eng, is_hi, 0, 0

            def up_to(self, count):
                while self.half < min(count, 2 * (C0 + HLB)):
                    j, half = self.half // 2, self.half % 2
                    if j == C0 + HL:
                        self.eng.wait_ge(half_used, 2 * C0)
                    elif j >= HL:
                        self.eng.wait_ge(half_used, 2 * (j - HL) + half + 1)
                    slot = j % HL if j < C0 else j - C0
                    if self.is_hi:
                        split_hi(self.eng, j % RAW, 16 * (j // RAW + 1), slot, (half,))
                    else:
                        split_lo(self.eng, j, j % RAW, slot, (half,))
                    self.half += 1

            def step(self, kind, j):
                if kind in CHUNKED:
                    self.chunk += 1
                    if (kind, j) != ("Q", 0):
                        self.up_to(2 * self.chunk + (2 if kind == "M" else AHEAD))

            def rest(self):
                self.up_to(2 * self.chunk + AHEAD)

        def first_half(i, s):
            return (i, 0) if isinstance(i, int) and i == 0 and s == 0 else (i, 3 * s - 1)

        def second_weights(i, s):
            return (i, 3 * s + 1)

        def number(r, place):
            return C0 + 3 * NE * r + 6 * place[0] + place[1]

        def lands_of(r, place):
            return 16 * (C0 // RAW + NE * r + 2 * place[0] + place[1] // RAW + 1)

        def expert_slot_free(eng, r, place):
            eng.wait_ge(chunk_done, number(r, place) - C0 - HLB + 1)

        def split_ahead(r, place):
            return isinstance(r, int) and isinstance(place[0], int) and number(r, place) - C0 < HLB

        def expert_hi(eng, r, place):
            if split_ahead(r, place):
                return
            expert_slot_free(eng, r, place)
            split_hi(eng, place[1] % RAW, lands_of(r, place), place[1] % HLB)

        def expert_lo(eng, r, place):
            if split_ahead(r, place):
                return
            expert_slot_free(eng, r, place)
            split_lo(eng, number(r, place), place[1] % RAW, place[1] % HLB)

        def nxt(place):
            return place[0], place[1] + 1

        block = stack.enter_context(nc.Block())

        @block.sync
        def _(sp):
            sp.dma_start(ident[:, :], consts[:, CONST_AT["ident"]:CONST_AT["ident"] + P]).then_inc(in_landed["vecs"], 16)
            sp.dma_start(vrow[0:8, :], c[0].rearrange("(k p) -> k p", p=P)).then_inc(in_landed["vecs"], 16)
            sp.dma_start(vrow[8:16, :], c_ctx.rearrange("(k p) -> k p", p=P)).then_inc(in_landed["vecs"], 16)
            sp.dma_start(vrow[16:24, :], norm1_w[0].rearrange("(k p) -> k p", p=P)).then_inc(in_landed["vecs"], 16)
            sp.dma_start(vrow[24:40, :], ret_gn_w[0].rearrange("(k p) -> k p", p=P)).then_inc(in_landed["vecs"], 16)
            sp.dma_start(vrow[40:64, :], conv_w[0].rearrange("t (k p) -> (t k) p", p=P)).then_inc(in_landed["vecs"], 16)
            sp.dma_start(xtok[:, 0:2, :], x[0].rearrange("(b p) n -> p b n", p=P)).then_inc(in_landed["x"], 16)
            sp.dma_start(xtok[:, 2:4, :], ctx_in[0].rearrange("(b p) n -> p b n", p=P)).then_inc(in_landed["ctx"], 16)
            for j, (kind, n) in enumerate(CHUNKS):
                if j >= RAW:
                    sp.wait_ge(lo_done, 2 * (j - RAW) + 2)
                wide_chunk, src = chunk_source(kind, n)
                dst = wide(raw[j % RAW]) if wide_chunk else raw[j % RAW][:, :, :]
                sp.dma_start(dst, src).then_inc(landed[j % RAW], 16)

            def load(r, place, src):
                slot = place[1] % RAW
                sp.wait_ge(lo_done, 2 * number(r, place) - 2 * RAW + 2)
                wide_chunk = src.shape[1] == 4
                sp.dma_start(wide(raw[slot]) if wide_chunk else raw[slot][:, :, :], src).then_inc(landed[slot], 16)

            def one_round(r):
                def expert(i, s):
                    e = 2 * i + s
                    p13 = first_half(i, s)
                    load(r, p13, w13_v[e][:, :, 0:512])
                    load(r, nxt(p13), w13_v[e][:, :, 512:1024])
                    if not (isinstance(e, int) and e == 0):
                        load(r, second_weights(i, s), w2_v[e - 1])

                for s in range(2):
                    expert(0, s)
                with sp.Fori(1, NE // 2) as i:
                    for s in range(2):
                        expert(i, s)
                load(r, (NE // 2 - 1, 5), w2_v[NE - 1])

            one_round(0)
            sp.wait_ge(routed, 1)
            rounds = sp.value_load(rounds_i[0:1, 0:1], min_val=1, max_val=4)
            with sp.If(rounds > 1):
                with sp.Fori(1, rounds) as r:
                    one_round(r)
            for b in range(2):
                sp.wait_ge(fin_ready, b + 1)
                sp.dma_start(out[0, b * P:(b + 1) * P, :], hx2[:, b, :]).then_inc(out_done, 16)
            sp.wait_ge(out_done, 32)

        @block.gpsimd
        def _(pool):
            for n, (tile, shape) in enumerate(CONSTS):
                dst = {"ident": ident, "rope": rope, "dist": dist, "slot_no": slot_no, "ident2": ident2, "desc": desc}.get(tile)
                if dst is None or dst is ident:
                    continue
                lo_col = CONST_AT[tile]
                src = consts[:, lo_col:lo_col + shape]
                flat = dst[:] if len(dst.shape) == 2 else dst[:].rearrange(
                    "p a t -> p (a t)" if len(dst.shape) == 3 else "p a b t -> p (a b t)")
                pool.dma_start(flat, src).then_inc(in_landed["consts"], 16)
            pool.dma_start(selc[:, :], consts[0:5, CONST_AT["selc"]:CONST_AT["selc"] + 2]).then_inc(in_landed["consts"], 16)
            pool.dma_start(selm[:, :], consts[0:40, CONST_AT["selm"]:CONST_AT["selm"] + 8]).then_inc(biases_landed, 16)
            pool.dma_start(lgd[:, :], ret_log_decay[0].rearrange("d h -> (d h)").partition_broadcast(P))\
                .then_inc(in_landed["decay"], 16)
            pool.memset(eps[:, 0:1], NORM_EPS)
            pool.memset(eps[:, 1:2], GN_EPS).then_inc(made, 1)
            for j in range(4):
                if j >= 2:
                    wait_pe(pool, ("MC", j - 2))
                pool.dma_start(mrow[4:5, j % 2, :], b_mod[0:1, 512 * j:512 * (j + 1)]).then_inc(brow_landed[j % 2], 16)
            wait_pe(pool, ("MC", 3))
            pool.dma_start(mstack[32:40, :], b_mod[0, 2048:].rearrange("(r n) -> r n", n=512)).then_inc(biases_landed, 16)
            for j in range(4, 12):
                pool.wait_ge(act_step, act_count(("M", j)))
                pool.dma_start(mstack[4 * (j - 4):4 * (j - 3), :], mrow[0:4, 0, :]).then_inc(stacked, 16)
            wait_pe(pool, ("GB", 1))
            pool.dma_start(xres[:, :, :], x[0].rearrange("(b p) n -> p b n", p=P)).then_inc(in_landed["xres"], 16)
            pool.wait_ge(dve_step, dve_count(("GB", 1)))
            pool.wait_ge(act_step, act_count(("GB", 1)))
            pool.dma_start(norm2[:, :], norm2_w[0].partition_broadcast(P)).then_inc(in_landed["norm2"], 16)
            pool.dma_start(rw[:, :, 0:NG], router_group_w[0].rearrange("(k p) n -> p k n", p=P)).then_inc(in_landed["router"], 16)
            pool.dma_start(rw[:, :, NG:], router_expert_w[0].rearrange("(k p) n -> p k n", p=P)).then_inc(in_landed["router"], 16)
            pool.dma_start(rbias[:, 0:NG], router_group_b[0].partition_broadcast(P)).then_inc(in_landed["router"], 16)
            pool.dma_start(rbias[:, NG:], router_expert_b[0].partition_broadcast(P)).then_inc(in_landed["router"], 16)
            pool.dma_start(tri[:, :], consts[:, CONST_AT["tri"]:CONST_AT["tri"] + P]).then_inc(in_landed["router"], 16)
            pool.dma_start(ones[:, :], consts[:, CONST_AT["ones"]:CONST_AT["ones"] + P]).then_inc(in_landed["router"], 16)
            pool.memset(zrow[:, :], 0.0).then_inc(made, 1)
            wait_pe(pool, ("MA", 11))
            pool.dma_start(finw[:, :], final_norm_w.partition_broadcast(P)).then_inc(in_landed["finw"], 16)

        @block.tensor
        def _(pe):
            def after(act=None, dve=None):
                if act is not None:
                    pe.wait_ge(act_step, act_count(act))
                if dve is not None:
                    pe.wait_ge(dve_step, dve_count(dve))

            chunk_no = [0]

            def next_chunk():
                chunk_no[0] += 1
                j = chunk_no[0] - 1
                return hi[j % HL], lo[j % HL]

            def rows_of(rows):
                for k in range(rows):
                    if k % (rows // 2) == 0:
                        pe.wait_ge(lo_done, 2 * chunk_no[0] - 1 + k // (rows // 2))
                    yield k

            def half_end(last, k, rows):
                if (k + 1) % (rows // 2) == 0:
                    last.then_inc(half_used, 1)

            def features_out(wh, wl, banks, operands, rows=8, tiles=4, halves_ready=None):
                for k in rows_of(rows):
                    if halves_ready is not None and k % 4 == 0:
                        pe.wait_ge(halves_ready, k // 4 + 1)
                    for f in range(tiles):
                        col = slice(f * P, (f + 1) * P)
                        for o, (xh, xl) in enumerate(operands):
                            dst = banks(f, o)
                            clears = k == 0 and (o == 0 if len(operands) == 2 else f % 2 == 0)
                            end = k == rows - 1
                            pe.matmul(dst, wh[:, k, col], xh[:, k, :], start=clears, stop=False, skip_group_check=True)
                            pe.matmul(dst, wh[:, k, col], xl[:, k, :], start=False, stop=False, skip_group_check=True)
                            last = pe.matmul(dst, wl[:, k, col], xh[:, k, :], start=False, stop=end, skip_group_check=True)
                    half_end(last, k, rows)
                return None

            def tokens_out(outs, wh, wl, halves_ready=None):
                for k in rows_of(8):
                    if halves_ready is not None and k % 4 == 0:
                        after(dve=halves_ready[k // 4])
                    for dst, stat_h, stat_l in outs:
                        pe.matmul(dst, stat_h(k), wh[:, k, :], start=(k == 0), stop=False)
                        pe.matmul(dst, stat_l(k), wh[:, k, :], start=False, stop=False)
                        last = pe.matmul(dst, stat_h(k), wl[:, k, :], start=False, stop=(k == 7))
                    half_end(last, k, 8)
                return None

            def token_block(dst, parts, b):
                return (dst, lambda k: parts[0][:, k, b * P:(b + 1) * P], lambda k: parts[1][:, k, b * P:(b + 1) * P])

            def half_banks(first):
                return lambda f, o: ps[:, first + f // 2, T * (f % 2):T * (f % 2 + 1)]

            for step in STEPS:
                kind, j = step
                if kind == "TV":
                    pe.wait_ge(in_landed["vecs"], 16 * 6)
                    last = pe.transpose(ps[:, 5, 0:64], vrow[:, :], ident[0:64, 0:64])
                elif kind == "XT":
                    if j == 0:
                        pe.wait_ge(xn_ready, 4)
                    if j == 1:
                        after(dve=("TV", 0))
                    if j == 2:
                        after(act=("XT", 0), dve=("XT", 0))
                    for k in ((0, 1, 2, 3), (4, 5), (6, 7))[j]:
                        for t in range(4):
                            last = pe.transpose(ps[:, k % 6, t * P:(t + 1) * P], xtok[:, t, k * P:(k + 1) * P], ident[:, :])
                elif kind == "M":
                    wh, wl = next_chunk()
                    if j >= 2:
                        pe.wait_ge(act_step, act_count(("M", j - 1)))
                    pe.wait_ge(silu_parts, 1)
                    bank = M_BANK.get(j, 6)
                    act_reader, dve_reader = {
                        5: (None, ("PV", 0)), 6: (("V", 1), None), 7: (None, ("PV", 1)),
                        8: (("K", 1), ("K", 1)), 9: (None, ("PV", 2)), 10: (("V", 3), None),
                        11: (None, ("PV", 3))}.get(j, (None, None))
                    after(act=act_reader, dve=dve_reader)
                    for k in rows_of(8):
                        pe.matmul(ps[0:4, bank, :], cs[:, k, :], wh[:, k, :], start=(k == 0), stop=False)
                        last = pe.matmul(ps[0:4, bank, :], cs[:, k, :], wl[:, k, :], start=False, stop=(k == 7))
                        half_end(last, k, 8)
                    last = None
                elif kind == "MC":
                    after(act=("M", j))
                    if j >= 1:
                        after(dve=("MC", j - 1))
                    pe.wait_ge(brow_landed[j % 2], 16 * (j // 2 + 1))
                    pe.wait_ge(in_landed["consts"], 16 * CONST_LOADS)
                    for f in range(4):
                        last = pe.matmul(ps[:, 7, 2 * f:2 * f + 2], mrow[0:5, j % 2, f * P:(f + 1) * P], selc[:, :],
                                         start=True, stop=True)
                elif kind in ("MB", "MA"):
                    pe.wait_ge(stacked, 16 * 8)
                    pe.wait_ge(biases_landed, 32)
                    bank, act_reader, dve_reader = {
                        4: (2, ("GB", 0), None), 5: (3, ("GB", 0), None), 6: (0, ("GB", 1), None),
                        7: (1, ("GB", 1), None), 8: (2, None, ("MB", 4)), 9: (3, None, ("MB", 5)),
                        10: (6, None, ("WO", 1)), 11: (7, None, ("WO", 1))}[j]
                    after(act=act_reader, dve=dve_reader)
                    last = pe.matmul(ps[:, bank, :], selm[:, j - 4:j - 3].broadcast_to([40, P]), mstack[:, :], start=True, stop=True)
                elif kind == "K":
                    wh, wl = next_chunk()
                    if j == 0:
                        pe.wait_ge(hx_lo, 3)
                    else:
                        after(act=("M", 6), dve=("V", 1))
                    last = features_out(wh, wl, lambda f, o: ps[:, f, T * o:T * (o + 1)],
                                        [(hxh, hxl), (hch, hcl)])
                elif kind == "Q":
                    wh, wl = next_chunk()
                    if j == 1:
                        after(dve=("RO", 1))
                    else:
                        after(act=("XT", 2), dve=("MC", 3))
                    last = features_out(wh, wl, half_banks(4), [(hxh, hxl)], halves_ready=hx_lo if j == 0 else None)
                elif kind == "V":
                    wh, wl = next_chunk()
                    prev = {0: ("K", 0), 1: ("V", 0), 2: ("K", 1), 3: ("V", 2)}[j]
                    after(act=("M", 8) if j == 2 else prev, dve=prev)
                    last = tokens_out([token_block(ps[:, t, :], (hxh, hxl) if t < 2 else (hch, hcl), t % 2)
                                       for t in range(4)], wh, wl)
                elif kind == "S":
                    after(act=("K", j // 2), dve=("K", 0) if j < 2 else ("Q", 1))
                    if j >= 1:
                        after(dve=("RO", j - 1))
                    for t in range(4):
                        for m in range(2):
                            f = 2 * (j % 2) + m
                            last = pe.matmul(ps[:, 4 + t // 2, T * (t % 2):T * (t % 2 + 1)],
                                             k_sb[:, f, t * P:(t + 1) * P], q_sb[:, f, :], start=(m == 0), stop=(m == 1))
                elif kind == "G":
                    wh, wl = next_chunk()
                    if j >= 1:
                        after(dve=("RO", j - 1))
                    else:
                        after(act=("M", 4))
                    last = features_out(wh, wl, half_banks(6), [(hxh, hxl)])
                elif kind == "PV":
                    after(act=("V", j), dve=("S", j))
                    for b in range(2):
                        for t in range(4):
                            last = pe.matmul(ps[:, 4 + b, :], att[:, t, b * P:(b + 1) * P], v_sb[:, t, :],
                                             start=(t == 0), stop=(t == 3))
                elif kind == "T":
                    after(act=("G", j), dve=("PV", j))
                    for e in range(4):
                        for b in range(2):
                            last = pe.transpose(ps[:, 6 + e // 2, T * (e % 2) + b * P:T * (e % 2) + (b + 1) * P],
                                                yn[:, b, e * P:(e + 1) * P], ident[:, :])
                elif kind in ("RO", "CO"):
                    wh, wl = next_chunk()
                    if kind == "RO":
                        after(act=("M", 5 + 2 * j), dve=("T", j))
                    else:
                        after(dve=("CB", j))
                        after(dve=("RO", 3) if j == 0 else ("CO", 0))
                    last = features_out(wide(wh), wide(wl), half_banks(4), [(yth, ytl)], rows=4, tiles=8)
                elif kind in ("CH", "CC", "CB", "GA", "GB"):
                    wh, wl = next_chunk()
                    first, prev_act, prev_dve = {
                        ("CH", 0): (0, ("K", 1), ("V", 3)), ("CC", 0): (2, ("V", 3), ("V", 3)),
                        ("CB", 0): (0, ("CH", 0), None), ("CH", 1): (0, None, None),
                        ("CC", 1): (2, None, ("CC", 0)), ("CB", 1): (0, ("CH", 1), None),
                        ("GA", 0): (2, None, ("CC", 1)), ("GA", 1): (0, None, None),
                        ("GB", 0): (2, ("GA", 0), None), ("GB", 1): (0, ("GA", 1), None)}[step]
                    after(act=prev_act, dve=prev_dve)
                    if step == ("CH", 0):
                        after(act=("M", 10))
                    if step in (("CH", 1), ("GA", 1)):
                        pe.wait_ge(prod_ready, H + 1 if kind == "CH" else H + 2)
                    last = features_out(wh, wl, half_banks(first), [(hxh, hxl)])
                elif kind == "WO":
                    wh, wl = next_chunk()
                    after(dve=("CO", 1))
                    last = tokens_out([token_block(ps[:, 4 + 2 * j + b, :], (hch, hcl), b) for b in range(2)], wh, wl,
                                      halves_ready=(("GB", 0), ("GB", 1)))
                elif kind == "HT":
                    after(act=("MA", 7), dve=("MB", 9))
                    for b in range(2):
                        pe.wait_ge(hx2_ready, b + 1)
                        for k in range(8):
                            last = pe.transpose(ps[:, k // 2, T * (k % 2) + b * P:T * (k % 2) + (b + 1) * P],
                                                hx2[:, b, k * P:(k + 1) * P], ident[:, :])
                elif kind == "LG":
                    after(act=("HT", 0), dve=("HT", 0))
                    pe.wait_ge(in_landed["router"], 96)
                    for b in range(2):
                        for k in range(8):
                            last = pe.matmul(ps[:, 4, 64 * b:64 * b + NG + NE], hx2T[:, k, b * P:(b + 1) * P],
                                             rw[:, k, :], start=(k == 0), stop=(k == 7))
                elif kind == "PS":
                    pe.wait_ge(made, 2)
                    for bank in range(4):
                        pe.matmul(ps[:, bank, :], zrow[0:1, 0:P], zrow[0:1, :], start=True, stop=False,
                                  skip_group_check=True)
                    after(dve=("LG", 0))
                    pe.matmul(ps[:, 5, 0:NE], tri[:, :], mask[:, 0, :], start=True, stop=True)
                    pe.matmul(ps[:, 5, NE:2 * NE], tri[:, :], mask[:, 1, :], start=True, stop=False)
                    pe.matmul(ps[:, 5, NE:2 * NE], ones[:, :], mask[:, 0, :], start=False, stop=True)
                    pe.matmul(ps[:, 5, 2 * NE:3 * NE], ones[:, :], mask[:, 0, :], start=True, stop=False)
                    last = pe.matmul(ps[:, 5, 2 * NE:3 * NE], ones[:, :], mask[:, 1, :], start=False, stop=True)
                if kind not in CHUNKED:
                    last.then_inc(pe_step, 1)

            after(act=("MA", 11), dve=("PS", 0))

            def one_round(r):
                n0, g0 = NE * r, (NE // 2) * r

                def gather(i):
                    pe.wait_ge(p_ready, g0 + i + 1)
                    for bank in range(2):
                        for k in range(4):
                            f = 4 * bank + k
                            for b in range(2):
                                last = pe.matmul(ps[:, 6 + bank, k * P:(k + 1) * P], hx2[:, b, f * P:(f + 1) * P],
                                                 pick[:, b, :], start=(b == 0), stop=(b == 1))
                        last.then_inc(g_full, 1)

                def first_product(i, s, n):
                    place = first_half(i, s)
                    for half in range(2):
                        j = number(r, place)
                        if half == 0:
                            if s == 0:
                                pe.wait_ge(x_hi, 2 * (g0 + i) + 2)
                                pe.wait_ge(x_lo, 2 * (g0 + i) + 2)
                            if not isinstance(n, int) or n > 0:
                                pe.wait_ge(act_ready, n)
                        elif not isinstance(n, int) or n > 0:
                            pe.wait_ge(sel_ready, n)
                            pe.wait_ge(cw_ready, n)
                        slot = place[1] % HLB
                        for k in range(8):
                            if k % 4 == 0:
                                pe.wait_ge(lo_done, 2 * j + k // 4 + 1)
                            pe.matmul(ps[:, 4 + half, :], xg[:, s, k, :], hi[slot][:, k, :], start=(k == 0), stop=False)
                            last = pe.matmul(ps[:, 4 + half, :], xg[:, s, k, :], lo[slot][:, k, :], start=False,
                                             stop=(k == 7))
                        last.then_inc(chunk_done, 1)
                        place = nxt(place)

                def scatter(n, s):
                    pe.wait_ge(y_lo, 2 * n + 2)
                    pe.wait_ge(sel_ready, n + 1)
                    for b in range(2):
                        for half in range(2):
                            for part in (yh, yl):
                                last = pe.matmul(ps[:, 2 * b + half, :], sel[:, s, b * P:(b + 1) * P],
                                                 part[:, half, :], start=False, stop=False, skip_group_check=True)
                    last.then_inc(s_done, 1)

                def turn(n, s):
                    pe.wait_ge(hs_ready, 2 * n + 2)
                    for f in range(8):
                        last = pe.matmul(ps[:, 4, f * CAP:(f + 1) * CAP], hs[:, f // 4, (f % 4) * P:(f % 4 + 1) * P],
                                         ident2[:, :], start=True, stop=True)
                    last.then_inc(t_full, 1)
                    pe.wait_ge(pw_ready, n + 1)
                    for b in range(2):
                        last = pe.transpose(ps[:, 5, b * P:(b + 1) * P], pickw[:, s, b, :], ident[:, :])
                    last.then_inc(pt_full, 1)

                def second_product(n, s, place, gathered):
                    j = number(r, place)
                    pe.wait_ge(act_ready, n + 1)
                    if gathered is not None:
                        pe.wait_ge(x_hi, gathered)
                        pe.wait_ge(x_lo, gathered)
                    if not isinstance(n, int) or n > 0:
                        pe.wait_ge(y_lo, 2 * n)
                    pe.wait_ge(lo_done, 2 * j + 2)
                    wh, wl = wide(hi[place[1] % HLB]), wide(lo[place[1] % HLB])
                    for half in range(2):
                        col = slice(half * 512, (half + 1) * 512)
                        for k in range(4):
                            pe.matmul(ps[:, 6 + half, :], actp[:, s, k, :], wh[:, k, col], start=(k == 0), stop=False)
                            last = pe.matmul(ps[:, 6 + half, :], actp[:, s, k, :], wl[:, k, col], start=False,
                                             stop=(k == 3))
                        last.then_inc(y_full if half == 0 else chunk_done, 1)

                def expert(i, s, head=False, tail=False):
                    n = n0 + 2 * i + s
                    first_product(i, s, n)
                    more = s == 1 and not tail
                    if more:
                        if not head:
                            pe.wait_ge(y_lo, 2 * n - 2)
                        gather(i + 1)
                    if not head:
                        scatter(n - 2, s)
                    turn(n, s)
                    if not (head and s == 0):
                        second_product(n - 1, 1 - s, second_weights(i, s), 2 * (g0 + i) + 4 if more else None)

                if not isinstance(r, int):
                    pe.wait_ge(y_lo, 2 * n0)
                gather(0)
                if isinstance(r, int):
                    pe.wait_ge(routed, 1)
                for s in range(2):
                    expert(0, s, head=True)
                with pe.Fori(1, NE // 2 - 1) as i:
                    for s in range(2):
                        expert(i, s)
                for s in range(2):
                    expert(NE // 2 - 1, s, tail=True)
                scatter(n0 + NE - 2, 0)
                second_product(n0 + NE - 1, 1, (NE // 2 - 1, 5), None)
                scatter(n0 + NE - 1, 1)

            one_round(0)
            pe.wait_ge(routed, 1)
            rounds = pe.value_load(rounds_i[0:1, 0:1], min_val=1, max_val=4)
            with pe.If(rounds > 1):
                with pe.Fori(1, rounds) as r:
                    one_round(r)

        @block.scalar
        def _(act):
            pe_at = lambda step: wait_pe(act, step)
            dve_at = lambda step: act.wait_ge(dve_step, dve_count(step))
            steps_done = [0]
            ch = Chain(act, act_chain)

            def done(ins):
                ins.then_inc(act_step, 1)
                steps_done[0] += 1
                act.wait_ge(act_step, steps_done[0])

            def preload(function):
                act.activation(loaded[:, :], eps[:, :], function).then_inc(act_chain, 1)
                ch.n += 1
                act.wait_ge(act_chain, ch.n)

            dve_at(("TV", 0))
            act.activation(csilu[:, :], cols[:, 0:16], ACT.Silu).then_inc(silu_ready, 1)
            act.wait_ge(made, 1)
            for t in range(4):
                act.wait_ge(in_landed["x" if t < 2 else "ctx"], 16)
                ch.link(act.activation(xnT[:, 0:2, :], xtok[:, t, :].rearrange("p (a n) -> p a n", a=2), ACT.Square,
                                       accum_out=stat[:, t:t + 1]))
            act.activation(stat[:, :], stat[:, :], ACT.Sqrt, scale=1.0 / D, bias=eps[:, 0:1]).then_inc(roots, 1)
            splits = MixerSplits(act, True)
            splits.up_to(2)
            for step in STEPS:
                kind, j = step
                splits.step(kind, j)
                if kind == "XT":
                    pe_at(step)
                    for n, k in enumerate(((0, 1), (4,), (6,))[j]):
                        last = act.activation(xnT[:, k, :], ps[:, k % 6, :], ACT.Copy)
                    done(last)
                elif kind == "M":
                    pe_at(step)
                    if j > 4:
                        act.wait_ge(stacked, 16 * (j - 4))
                    done(act.activation(mrow[0:4, j % 2 if j < 4 else 0, :], ps[0:4, M_BANK.get(j, 6), :], ACT.Copy))
                    splits.rest()
                elif kind == "MA":
                    if j == 6:
                        dve_at(("WO", 0))
                        for b in range(2):
                            ch.link(act.activation(hx2T[:, 0:2, :].rearrange("p a n -> p (a n)"), x1[:, b, 0:512],
                                                   ACT.Square, accum_out=stat[:, b:b + 1]))
                        ch.link(act.activation(stat[:, 0:2], stat[:, 0:2], ACT.Identity, scale=1.0 / D, bias=eps[:, 0:1]))
                        preload(ACT.Sqrt)
                    pe_at(step)
                    col = slice(512 * (j % 2), 512 * (j % 2) + 512)
                    dst, bank = {6: (shift2, 0), 7: (shift2, 1), 10: (gate2, 6), 11: (gate2, 7)}[j]
                    done(act.activation(dst[:, col], ps[:, bank, :], ACT.Copy))
                elif kind == "Q" and j == 0:
                    for n in range(2):
                        act.wait_ge(hx_mod, n + 1)
                        act.activation(hxh[:, 4 * n:4 * n + 4, :], xnT[:, 4 * n:4 * n + 4, 0:T], ACT.Copy).then_inc(hx_hi, 1)
                    for k in range(4):
                        last = act.activation(xnT[:, k, T:2 * T], xnT[:, k, T:2 * T], ACT.Identity,
                                              scale=s1[:, k, 1:2], bias=modc[:, k, 1:2])
                    ch.link(last)
                    act.wait_ge(hx_mod, 3)
                    act.activation(hch[:, :, :], xnT[:, :, T:2 * T], ACT.Copy).then_inc(hx_hi, 1)
                    splits.rest()
                elif kind == "K":
                    if j == 0:
                        act.wait_ge(in_landed["decay"], 16)
                        ch.link(act.activation(lgt[:, 0, :], lgd[:, :], ACT.Exp))
                        ch.link(act.activation(lgt[:, 1, :], lgt[:, 0, :], ACT.Copy, scale=-1.0, bias=1.0))
                        act.activation(lgt[:, 2, :], lgt[:, 1, :], ACT.Ln).then_inc(log_ready, 1)
                    pe_at(step)
                    done(act.activation(k_sb[:, :, T:2 * T], ps[:, 0:4, T:2 * T], ACT.Copy))
                elif kind == "V":
                    pe_at(step)
                    if j == 0:
                        dve_at(("K", 0))
                    done(act.activation(v_sb[:, 0:2, :], ps[:, 0:2, :], ACT.Copy))
                elif kind == "S":
                    act.wait_ge(darg_ready, j + 1)
                    f, b = j, H + j
                    act.activation(att[:, 2:4, :], dist[:, :, :], ACT.Exp, scale=lgt[:, 0, f:f + 1], bias=lgt[:, 2, f:f + 1])
                    act.activation(g_sb[:, 0:2, :], dist[:, :, :], ACT.Exp, scale=lgt[:, 1, b:b + 1], bias=lgt[:, 2, b:b + 1])
                    done(act.activation(att[:, 0:2, :], darg[:, :, :], ACT.Exp))
                elif kind == "G":
                    pe_at(step)
                    dve_at(("S", j))
                    done(act.activation(g_sb[:, :, :], ps[:, 6:8, :].rearrange("p a (b t) -> p (a b) t", b=2), ACT.Silu))
                elif kind == "PV":
                    act.wait_ge(gvar_ready, j + 1)
                    done(act.activation(grs[:, :], gmv[:, :, 1], ACT.Sqrt, bias=eps[:, 1:2]))
                elif kind == "T":
                    act.wait_ge(prod_ready, j + 1)
                    done(act.activation(yth[:, :, :], g_sb[:, :, :], ACT.Copy))
                elif kind == "CH":
                    pe_at(step)
                    if j == 1:
                        dve_at(("CC", 0))
                    done(act.activation(ch_sb[:, :, :], ps[:, 0:2, :].rearrange("p a (b t) -> p (a b) t", b=2), ACT.Copy))
                elif kind == "CB":
                    act.wait_ge(prod_ready, H + j + 1)
                    done(act.activation(yth[:, :, :], conv_sb[:, :, :], ACT.Copy))
                elif kind in ("GA", "GB"):
                    pe_at(step)
                    dve_at({("GA", 0): ("CB", 1), ("GA", 1): ("GA", 0), ("GB", 0): ("GA", 1), ("GB", 1): ("GB", 0)}[step])
                    first = {("GA", 0): 2, ("GA", 1): 0, ("GB", 0): 2, ("GB", 1): 0}[step]
                    sig = act.activation(g_sb[:, :, :], ps[:, first:first + 2, :].rearrange("p a (b t) -> p (a b) t", b=2),
                                         ACT.Sigmoid)
                    if kind == "GA":
                        done(sig)
                    else:
                        sig.then_inc(gates_ready, 1)
                        act.wait_ge(prod_ready, H + 2 + j + 1)
                        done(act.activation(hch[:, 4 * j:4 * j + 4, :], racc[:, 4 * j:4 * j + 4, :], ACT.Copy))
                elif kind == "HT":
                    dve_at(("WO", 1))
                    for b in range(2):
                        ch.link(act.activation(hx2T[:, 0:2, :].rearrange("p a n -> p (a n)"), x1[:, b, 512:], ACT.Square,
                                               accum_out=stat[:, 2 + b:3 + b]))
                    for b in range(2):
                        act.activation(stat[:, 2 + b:3 + b], stat[:, 2 + b:3 + b], ACT.Sqrt, scale=1.0 / D,
                                       bias=stat[:, b:b + 1]).then_inc(roots, 1)
                    splits.up_to(2 * C0 + 5)
                    preload(ACT.Exp)
                    pe_at(step)
                    done(act.activation(hx2T[:, 0:4, :].rearrange("p (a b) t -> p a (b t)", b=2), ps[:, 0:2, :], ACT.Copy))
                elif kind == "LG":
                    splits.up_to(2 * C0 + 6)
                    act.wait_ge(logit_ready, 1)
                    done(act.activation(rt[:, :, 80:85], rt[:, :, 72:77], ACT.Exp))
                    preload(ACT.Silu)

            def one_round(r):
                n0, g0 = NE * r, (NE // 2) * r

                def gathered_hi(i):
                    for bank in range(2):
                        act.wait_ge(g_full, 2 * (g0 + i) + bank + 1)
                        act.activation(xg[:, :, 4 * bank:4 * bank + 4, 0:CAP].rearrange("p s k c -> p k s c"),
                                       ps[:, 6 + bank, :].rearrange("p (k s c) -> p k s c", k=4, s=2),
                                       ACT.Copy).then_inc(x_hi, 1)

                def rows_hi(n, s, w2_place):
                    act.wait_ge(cw_ready, n + 1)
                    if not isinstance(n, int) or n > 0:
                        act.wait_ge(s_done, n)
                    for half in range(2):
                        if half == 0:
                            act.wait_ge(y_full, n + 1)
                        else:
                            act.wait_ge(chunk_done, number(r, w2_place) - C0 + 1)
                        act.activation(yh[:, half, :], ps[:, 6 + half, :], ACT.Copy, scale=cw[:, s:s + 1])\
                           .then_inc(y_hi, 1)

                def expert(i, s, head=False, tail=False):
                    n = n0 + 2 * i + s
                    if not head:
                        rows_hi(n - 2, s, (i, 3 * s - 2))
                    if not head:
                        expert_hi(act, r, second_weights(i, s))
                    last_one = tail and s == 1
                    first = head and s == 0
                    coming = first_half(i + s, 1 - s)
                    for half in range(2):
                        act.wait_ge(chunk_done, number(r, first_half(i, s)) - C0 + half + 1)
                        if half == 0 and (not isinstance(n, int) or n > 0):
                            act.wait_ge(t_full, n)
                            act.wait_ge(hs_ready, 2 * n)
                        act.activation(hs[:, half, :], ps[:, 4 + half, :], ACT.Copy).then_inc(hs_ready, 1)
                        if half == 0 and not last_one:
                            expert_hi(act, r, coming)
                            if first:
                                expert_hi(act, r, nxt(coming))
                    if s == 1 and not tail:
                        gathered_hi(i + 1)
                    act.wait_ge(t_full, n + 1)
                    if not isinstance(n, int) or n > 0:
                        act.wait_ge(act_ready, n)
                    act.activation(sa[:, :, :], ps[:, 4, 0:4 * CAP].rearrange("p (f c) -> p f c", f=4), ACT.Silu)\
                       .then_inc(sa_ready, 1)
                    act.wait_ge(pt_full, n + 1)
                    if not isinstance(n, int) or n > 1:
                        act.wait_ge(s_done, n - 1)
                    act.activation(sel[:, s, :], ps[:, 5, 0:T], ACT.Sign).then_inc(sel_ready, 1)
                    act.activation(wsum[:, :], ps[:, 5, 0:T], ACT.Copy, accum_out=cw[:, s:s + 1]).then_inc(cw_ready, 1)
                    if first:
                        expert_hi(act, r, second_weights(0, 1))
                    elif not last_one:
                        expert_hi(act, r, nxt(coming))

                expert_hi(act, r, (0, 0))
                gathered_hi(0)
                expert_hi(act, r, (0, 1))
                for s in range(2):
                    expert(0, s, head=True)
                with act.Fori(1, NE // 2 - 1) as i:
                    for s in range(2):
                        expert(i, s)
                for s in range(2):
                    expert(NE // 2 - 1, s, tail=True)
                rows_hi(n0 + NE - 2, 0, second_weights(NE // 2 - 1, 1))
                expert_hi(act, r, (NE // 2 - 1, 5))
                rows_hi(n0 + NE - 1, 1, (NE // 2 - 1, 5))

            one_round(0)
            act.wait_ge(routed, 1)
            rounds = act.value_load(rounds_i[0:1, 0:1], min_val=1, max_val=4)
            with act.If(rounds > 1):
                with act.Fori(1, rounds) as r:
                    one_round(r)
            preload(ACT.Sqrt)
            for b in range(2):
                act.wait_ge(squares, b + 1)
                act.activation(hs[:, :, :].rearrange("p a n -> p (a n)"), hx2[:, b, :], ACT.Square,
                               accum_out=stat[:, 2 + b:3 + b]).then_inc(act_chain, 1)
                ch.n += 1
                act.wait_ge(act_chain, ch.n)
                act.activation(stat[:, 2 + b:3 + b], stat[:, 2 + b:3 + b], ACT.Sqrt, scale=1.0 / D, bias=eps[:, 0:1])\
                   .then_inc(roots, 1)

        @block.vector
        def _(dve):
            pe_at = lambda step: wait_pe(dve, step)
            act_at = lambda step: dve.wait_ge(act_step, act_count(step))
            steps_done = [0]
            ch = Chain(dve, dve_chain)
            L = ch.link
            V = dve

            def done(ins):
                ins.then_inc(dve_step, 1)
                steps_done[0] += 1
                dve.wait_ge(dve_step, steps_done[0])

            def quad(first):
                return ps[:, first:first + 2, :].rearrange("p a (b t) -> p (a b) t", b=2)

            pe_at(("TV", 0))
            done(V.tensor_copy(cols[:, :], ps[:, 5, 0:64]))
            V.wait_ge(silu_ready, 1)
            cv = csilu[:, :].rearrange("p (v k) -> p k v", v=2)
            L(V.tensor_copy(cs[:, :, 0:2], cv))
            V.tensor_tensor(cs[:, :, 2:4], cv, cs[:, :, 0:2], ALU.subtract).then_inc(silu_parts, 1)
            V.wait_ge(roots, 1)
            L(V.reciprocal(stat[:, :], stat[:, :]))
            for t in range(4):
                V.tensor_scalar(xtok[:, t, :], xtok[:, t, :], stat[:, t:t + 1], None, ALU.mult).then_inc(xn_ready, 1)
            V.wait_ge(xn_ready, 4)
            splits = MixerSplits(dve, False)
            splits.up_to(2)
            for step in DVE_STEPS:
                kind, j = step
                if kind == "TV":
                    continue
                if step == ("T", 1):
                    splits.step("K", 1)
                elif step != ("K", 1):
                    splits.step(kind, j)
                if kind == "XT":
                    pe_at(step)
                    for k in ((2, 3), (5,), (7,))[j]:
                        last = V.tensor_copy(xnT[:, k, :], ps[:, k % 6, :])
                    done(last)
                elif kind == "MC":
                    pe_at(step)
                    done(V.tensor_copy(modc[:, 4 * j:4 * j + 4, :], ps[:, 7, 0:8].rearrange("p (f v) -> p f v", v=2)))
                elif kind == "MB":
                    pe_at(step)
                    src = ps[:, 2 + j % 2, :]
                    col = slice(512 * (j % 2), 512 * (j % 2) + 512)
                    if j in (8, 9):
                        V.wait_ge(in_landed["norm2"], 16)
                        done(V.scalar_tensor_tensor(scale2[:, col], src, 1.0, norm2[:, col], ALU.add, ALU.mult))
                    else:
                        done(V.tensor_copy(gate1[:, col], src))
                if step == ("Q", 0):
                    for v in range(2):
                        last = V.scalar_tensor_tensor(s1[:, :, v], modc[:, 8:16, v], 1.0, cols[:, 16:24], ALU.add, ALU.mult)
                    L(last)
                    act_at(("XT", 2))

                    def modulate(first, v):
                        for k in range(first, first + 4):
                            part = xnT[:, k, T * v:T * v + T]
                            last = V.tensor_scalar(part, part, s1[:, k, v:v + 1], modc[:, k, v:v + 1], ALU.mult, ALU.add)
                        last.then_inc(hx_mod, 1)

                    modulate(0, 0)
                    modulate(4, 0)
                    for n in range(2):
                        k = slice(4 * n, 4 * n + 4)
                        V.wait_ge(hx_mod, n + 1)
                        V.wait_ge(hx_hi, n + 1)
                        V.tensor_tensor(hxl[:, k, :], xnT[:, k, 0:T], hxh[:, k, :], ALU.subtract).then_inc(hx_lo, 1)
                    modulate(4, 1)
                    V.wait_ge(hx_mod, 3)
                    V.wait_ge(hx_hi, 3)
                    V.tensor_tensor(hcl[:, :, :], xnT[:, :, T:2 * T], hch[:, :, :], ALU.subtract).then_inc(hx_lo, 1)
                    V.wait_ge(in_landed["consts"], 16 * CONST_LOADS)
                    splits.rest()
                if kind in ("K", "Q"):
                    pe_at(step)
                    if kind == "K":
                        act_at(step)
                        src, dst, tmp = ps[:, 0:4, 0:T], k_sb[:, :, 0:T], att if j == 0 else q_sb
                        half = lambda lo_p, hi_p: ps[lo_p:hi_p, 0:4, 0:T]
                    else:
                        src, dst, tmp = quad(4), q_sb[:, :, :], att
                        half = lambda lo_p, hi_p: ps[lo_p:hi_p, 4:6, :].rearrange("p a (b t) -> p (a b) t", b=2)
                    two = lambda a: a.rearrange("p (h a) t -> p h a t", a=2)
                    for hh in range(2):
                        t2 = slice(2 * hh, 2 * hh + 2)
                        V.tensor_tensor(dst[:, t2, :], src[:, t2, :], rope[:, 0, :, :], ALU.mult)
                        V.tensor_tensor(tmp[0:64, t2, :], half(64, 128)[:, t2, :], rope[64:128, 1, :, :], ALU.mult)
                        last = V.tensor_tensor(tmp[64:128, t2, :], half(0, 64)[:, t2, :], rope[0:64, 1, :, :], ALU.mult)
                    L(last)
                    done(V.tensor_tensor(dst, dst, tmp[:, :, :], ALU.add))
                elif kind == "V":
                    if j == 0:
                        V.wait_ge(log_ready, 1)
                        e, u, ln = lgt[:, 0, :], lgt[:, 1, :], lgt[:, 2, :]
                        L(V.tensor_scalar(lgt[:, 3, :], u, 1.0, None, ALU.subtract))
                        L(V.reciprocal(lgt[:, 3, :], lgt[:, 3, :]))
                        L(V.tensor_tensor(lgt[:, 3, :], lgt[:, 3, :], e, ALU.mult))
                        L(V.tensor_scalar(lgt[:, 3, :], lgt[:, 3, :], -1.0, None, ALU.mult))
                        L(V.tensor_tensor(lgt[:, 0, :], lgt[:, 3, :], ln, ALU.mult))
                        L(V.tensor_scalar(lgt[:, 1, :], lgt[:, 0, :], -1.0, None, ALU.mult))
                        L(V.tensor_scalar(lgt[:, 2, :], lgt[:, 0, :], float(T), None, ALU.mult))
                    pe_at(step)
                    if j > 0:
                        pe_at(("PV", j - 1))
                    done(V.tensor_copy(v_sb[:, 2:4, :], ps[:, 2:4, :]))
                elif kind == "S":
                    if j > 0:
                        pe_at(("T", j - 1))
                    lf, nlb = lgt[:, 0, j:j + 1], lgt[:, 1, H + j:H + j + 1]
                    V.tensor_scalar(darg[:, :, :], dist[:, :, :], 0.0, lf, ALU.max, ALU.mult)
                    L(V.tensor_scalar(att[:, 0:2, :], dist[:, :, :], 0.0, nlb, ALU.min, ALU.mult))
                    V.tensor_tensor(darg[:, :, :], darg[:, :, :], att[:, 0:2, :], ALU.add).then_inc(darg_ready, 1)
                    act_at(step)
                    L(V.tensor_tensor(att[:, 2:4, :], att[:, 2:4, :], g_sb[:, 0:2, :], ALU.add))
                    pe_at(step)
                    done(V.scalar_tensor_tensor(att[:, :, :], quad(4), QK ** -0.5, att[:, :, :], ALU.mult, ALU.mult))
                elif kind == "PV":
                    pe_at(step)
                    for b in range(2):
                        last = V.bn_stats(gst[:, b, :], ps[:, 4 + b, :])
                    L(last)
                    for b in range(2):
                        last = V.bn_aggr(gmv[:, b, :], gst[:, b, :])
                    last.then_inc(gvar_ready, 1)
                    act_at(step)
                    L(V.reciprocal(grs[:, :], grs[:, :]))
                    for b in range(2):
                        last = V.tensor_scalar(yn[:, b, :], ps[:, 4 + b, :], gmv[:, b, 0:1], grs[:, b:b + 1],
                                               ALU.subtract, ALU.mult)
                    done(last)
                elif kind == "T":
                    pe_at(step)
                    act_at(("G", j))
                    for e in range(4):
                        n = 24 + 4 * j + e
                        last = V.scalar_tensor_tensor(g_sb[:, e, :], ps[:, 6 + e // 2, T * (e % 2):T * (e % 2 + 1)],
                                                      cols[:, n:n + 1], g_sb[:, e, :], ALU.mult, ALU.mult)
                    last.then_inc(prod_ready, 1)
                    act_at(step)
                    done(V.tensor_tensor(ytl[:, :, :], g_sb[:, :, :], yth[:, :, :], ALU.subtract))
                elif kind in ("RO", "CO"):
                    pe_at(step)
                    acc = (racc if kind == "RO" else cacc)[:, :, :].rearrange("p (a b) t -> p a (b t)", b=2)
                    if j == 0:
                        done(V.tensor_copy(acc, ps[:, 4:8, :]))
                    else:
                        done(V.tensor_tensor(acc, acc, ps[:, 4:8, :], ALU.add))
                elif kind == "CC":
                    pe_at(step)
                    act_at(("CH", j))
                    L(V.tensor_tensor(u_sb[:, :, :], quad(2), ch_sb[:, :, :], ALU.mult))
                    grid = lambda t, f: t[:, f, :].rearrange("p (r c) -> p r c", c=GRID)
                    tap = lambda n, f: cols[:, 40 + 8 * n + 4 * j + f:41 + 8 * n + 4 * j + f]
                    for f in range(4):
                        last = V.tensor_scalar(conv_sb[:, f, :], u_sb[:, f, :], tap(1, f), None, ALU.mult)
                    L(last)
                    for n, to, frm in ((0, slice(1, GRID), slice(0, GRID - 1)), (2, slice(0, GRID - 1), slice(1, GRID))):
                        for f in range(4):
                            last = V.scalar_tensor_tensor(grid(conv_sb, f)[:, :, to], grid(u_sb, f)[:, :, frm], tap(n, f),
                                                          grid(conv_sb, f)[:, :, to], ALU.mult, ALU.add)
                        if n == 0:
                            L(last)
                    done(last)
                elif kind == "CB":
                    pe_at(step)
                    V.tensor_tensor(conv_sb[:, :, :], quad(0), conv_sb[:, :, :], ALU.mult).then_inc(prod_ready, 1)
                    act_at(step)
                    V.wait_ge(prod_ready, H + j + 1)
                    done(V.tensor_tensor(ytl[:, :, :], conv_sb[:, :, :], yth[:, :, :], ALU.subtract))
                elif kind == "GA":
                    act_at(step)
                    part = racc[:, 4 * j:4 * j + 4, :]
                    done(V.tensor_tensor(part, part, g_sb[:, :, :], ALU.mult))
                elif kind == "GB":
                    V.wait_ge(gates_ready, j + 1)
                    ra, ca = racc[:, 4 * j:4 * j + 4, :], cacc[:, 4 * j:4 * j + 4, :]
                    L(V.tensor_tensor(ca, ca, g_sb[:, :, :], ALU.mult))
                    V.tensor_tensor(ra, ra, ca, ALU.add).then_inc(prod_ready, 1)
                    act_at(step)
                    V.wait_ge(prod_ready, H + 2 + j + 1)
                    done(V.tensor_tensor(hcl[:, 4 * j:4 * j + 4, :], ra, hch[:, 4 * j:4 * j + 4, :], ALU.subtract))
                elif kind == "WO":
                    pe_at(step)
                    V.wait_ge(in_landed["xres"], 16)
                    col = slice(512 * j, 512 * j + 512)
                    for b in range(2):
                        last = V.tensor_tensor(x1[:, b, col], ps[:, 4 + 2 * j + b, :], gate1[:, col], ALU.mult)
                    L(last)
                    done(V.tensor_tensor(x1[:, :, col], x1[:, :, col], xres[:, :, col], ALU.add))
                elif kind == "HT":
                    splits.up_to(2 * C0 + 4)
                    V.wait_ge(roots, 3)
                    act_at(("MA", 7))
                    L(V.reciprocal(stat[:, 0:2], stat[:, 2:4]))
                    for b in range(2):
                        L(V.scalar_tensor_tensor(hx2[:, b, :], x1[:, b, :], stat[:, b:b + 1], scale2[:, :], ALU.mult, ALU.mult))
                        V.tensor_tensor(hx2[:, b, :], hx2[:, b, :], shift2[:, :], ALU.add).then_inc(hx2_ready, 1)
                    splits.up_to(2 * C0 + 5)
                    pe_at(step)
                    done(V.tensor_copy(hx2T[:, 4:8, :].rearrange("p (a b) t -> p a (b t)", b=2), ps[:, 2:4, :]))
                elif kind == "LG":
                    splits.up_to(2 * C0 + 6)
                    pe_at(step)
                    V.wait_ge(in_landed["router"], 96)
                    R = lambda a, b: rt[:, :, a:b]
                    B = lambda t, n: t.to_broadcast([P, 2, n])
                    first_of = desc[:, :].unsqueeze(1).to_broadcast([P, 2, 8])
                    L(V.tensor_tensor(lg[:, :, :], ps[:, 4, 0:128].rearrange("p (b n) -> p b n", b=2)[:, :, 0:NG + NE],
                                      rbias[:, :].unsqueeze(1).to_broadcast([P, 2, NG + NE]), ALU.add))

                    def top(values, n, m, key, at_key):
                        L(V.reduce_max(m, values, AX.X))
                        L(V.tensor_tensor(key, values, B(m, n), ALU.is_equal))
                        L(V.tensor_tensor(key, key, first_of[:, :, 0:n], ALU.mult))
                        L(V.reduce_max(at_key, key, AX.X))
                        L(V.tensor_tensor(key, key, B(at_key, n), ALU.is_equal))

                    Lg = lg[:, :, 0:NG]
                    Le = lg[:, :, NG:].rearrange("p b (g e) -> p b g e", g=NG)
                    top(Lg, NG, R(0, 1), R(4, 8), R(1, 2))
                    group = R(4, 8).unsqueeze(3).to_broadcast([P, 2, NG, EPG])
                    L(V.tensor_tensor(R(16, 48).rearrange("p b (g e) -> p b g e", g=NG), Le, group, ALU.mult))
                    L(V.reduce_sum(R(8, 16), R(16, 48).rearrange("p b (g e) -> p b e g", g=NG), AX.X))
                    top(R(8, 16), EPG, R(2, 3), R(48, 56), R(1, 2))
                    L(V.scalar_tensor_tensor(R(56, 64), R(48, 56), -BIG, R(8, 16), ALU.mult, ALU.add))
                    top(R(56, 64), EPG, R(3, 4), R(64, 72), R(1, 2))
                    V.tensor_tensor(R(72, 76), Lg, B(R(0, 1), NG), ALU.subtract)
                    V.tensor_tensor(R(76, 77), R(3, 4), R(2, 3), ALU.subtract).then_inc(logit_ready, 1)
                    act_at(step)
                    L(V.reduce_sum(R(85, 86), R(80, 84), AX.X))
                    L(V.tensor_scalar(R(86, 87), R(84, 85), 1.0, None, ALU.add))
                    L(V.tensor_tensor(R(86, 87), R(86, 87), R(85, 86), ALU.mult))
                    L(V.reciprocal(R(87, 88), R(86, 87)))
                    L(V.tensor_tensor(R(88, 89), R(87, 88), R(84, 85), ALU.mult))
                    L(V.tensor_tensor(R(8, 16), R(48, 56), B(R(87, 88), 8), ALU.mult))
                    L(V.tensor_tensor(R(56, 64), R(64, 72), B(R(88, 89), 8), ALU.mult))
                    L(V.tensor_tensor(R(8, 16), R(8, 16), R(56, 64), ALU.add))
                    L(V.tensor_tensor(R(48, 56), R(48, 56), R(64, 72), ALU.add))
                    for src, dst in ((R(8, 16), combx[:, :, 0:NE]), (R(48, 56), mask[:, :, :])):
                        last = V.tensor_tensor(dst.rearrange("p b (g e) -> p b g e", g=NG),
                                               src.unsqueeze(2).to_broadcast([P, 2, NG, EPG]), group, ALU.mult)
                    done(last)
                elif kind == "PS":
                    pe_at(step)
                    L(V.scalar_tensor_tensor(posx[:, :, 0:NE], ps[:, 5, 0:2 * NE].rearrange("p (b e) -> p b e", b=2), 1.0,
                                             mask[:, :, :], ALU.add, ALU.mult))
                    L(V.tensor_scalar(posx[:, :, 0:NE], posx[:, :, 0:NE], 1.0, None, ALU.subtract))
                    done(V.nop())

            def count_rounds():
                for q in range(1, 4):
                    V.tensor_scalar(posx[:, :, q * NE:(q + 1) * NE], posx[:, :, 0:NE], float(CAP * q), None, ALU.subtract)
                    V.tensor_copy(combx[:, :, q * NE:(q + 1) * NE], combx[:, :, 0:NE])
                L(V.reduce_max(rmax[:, 0:1], ps[:, 5, 2 * NE:3 * NE], AX.X))
                L(V.tensor_scalar(rmax[:, 1:2], rmax[:, 0:1], float(CAP), 1.0, ALU.is_gt, ALU.add))
                for q in (2, 3):
                    L(V.scalar_tensor_tensor(rmax[:, 1:2], rmax[:, 0:1], float(CAP * q), rmax[:, 1:2], ALU.is_gt, ALU.add))
                V.tensor_copy(rounds_i[0:1, 0:1], rmax[0:1, 1:2]).then_inc(routed, 1)
                V.wait_ge(routed, 1)

            def one_round(r):
                n0, g0 = NE * r, (NE // 2) * r

                def pick_pair(i):
                    if not isinstance(r, int) or not isinstance(i, int) or i > 0:
                        V.wait_ge(g_full, 2 * (g0 + i))
                    for s in range(2):
                        for b in range(2):
                            last = V.tensor_scalar(pick[:, b, CAP * s:CAP * (s + 1)], slot_no[:, 0:CAP],
                                                   posx[:, b, bass.ds(n0 + 2 * i + s, 1)], None, ALU.is_equal)
                    last.then_inc(p_ready, 1)

                def weigh(i, s):
                    n = n0 + 2 * i + s
                    if not isinstance(n, int) or n >= 2:
                        V.wait_ge(pt_full, n - 1)
                    for b in range(2):
                        last = V.tensor_scalar(pickw[:, s, b, :], slot_no[:, :], posx[:, b, bass.ds(n, 1)],
                                               combx[:, b, bass.ds(n, 1)], ALU.is_equal, ALU.mult)
                    last.then_inc(pw_ready, 1)

                def gathered_lo(i):
                    for bank in range(2):
                        V.wait_ge(x_hi, 2 * (g0 + i) + bank + 1)
                        k = slice(4 * bank, 4 * bank + 4)
                        V.tensor_tensor(xg[:, :, k, CAP:P].rearrange("p s k c -> p k s c"),
                                        ps[:, 6 + bank, :].rearrange("p (k s c) -> p k s c", k=4, s=2),
                                        xg[:, :, k, 0:CAP].rearrange("p s k c -> p k s c"), ALU.subtract).then_inc(x_lo, 1)

                def rows_lo(n, s):
                    for half in range(2):
                        V.wait_ge(y_hi, 2 * n + half + 1)
                        V.scalar_tensor_tensor(yl[:, half, :], ps[:, 6 + half, :], cw[:, s:s + 1], yh[:, half, :],
                                               ALU.mult, ALU.subtract).then_inc(y_lo, 1)

                def expert(i, s, head=False, tail=False):
                    n = n0 + 2 * i + s
                    if not head:
                        rows_lo(n - 2, s)
                    if not head:
                        expert_lo(dve, r, second_weights(i, s))
                    last_one = tail and s == 1
                    first = head and s == 0
                    coming = first_half(i + s, 1 - s)
                    if not last_one:
                        expert_lo(dve, r, coming)
                    if first:
                        expert_lo(dve, r, nxt(coming))
                    if s == 1 and not tail:
                        gathered_lo(i + 1)
                    if s == 0 and not tail:
                        pick_pair(i + 1)
                    V.wait_ge(sa_ready, n + 1)
                    if not isinstance(n, int) or n > 1:
                        V.wait_ge(y_lo, 2 * n - 2)
                    if not isinstance(n, int) or n > 0:
                        V.wait_ge(act_ready, n)
                    up = ps[:, 4, 4 * CAP:8 * CAP].rearrange("p (f c) -> p f c", f=4)
                    V.tensor_tensor(actp[:, s, :, 0:CAP], up, sa[:, :, :], ALU.mult)
                    V.tensor_tensor(am[:, :, :], up, sa[:, :, :], ALU.mult).then_inc(am_ready, 1)
                    V.wait_ge(am_ready, n + 1)
                    V.tensor_tensor(actp[:, s, :, CAP:P], am[:, :, :], actp[:, s, :, 0:CAP], ALU.subtract).then_inc(act_ready, 1)
                    if not last_one:
                        expert_lo(dve, r, second_weights(0, 1) if first else nxt(coming))
                        weigh(i + s, 1 - s)

                pick_pair(0)
                weigh(0, 0)
                if isinstance(r, int):
                    count_rounds()
                expert_lo(dve, r, (0, 0))
                gathered_lo(0)
                expert_lo(dve, r, (0, 1))
                for s in range(2):
                    expert(0, s, head=True)
                with dve.Fori(1, NE // 2 - 1) as i:
                    for s in range(2):
                        expert(i, s)
                for s in range(2):
                    expert(NE // 2 - 1, s, tail=True)
                rows_lo(n0 + NE - 2, 0)
                expert_lo(dve, r, (NE // 2 - 1, 5))
                rows_lo(n0 + NE - 1, 1)
                V.wait_ge(s_done, n0 + NE)

            one_round(0)
            dve.wait_ge(routed, 1)
            rounds = dve.value_load(rounds_i[0:1, 0:1], min_val=1, max_val=4)
            with dve.If(rounds > 1):
                with dve.Fori(1, rounds) as r:
                    one_round(r)
            dve.wait_ge(in_landed["finw"], 16)
            for b in range(2):
                L(V.tensor_tensor(hx2[:, b, :], ps[:, 2 * b:2 * b + 2, :].rearrange("p a n -> p (a n)"), gate2[:, :], ALU.mult))
                V.tensor_tensor(hx2[:, b, :], hx2[:, b, :], x1[:, b, :], ALU.add).then_inc(squares, 1)
            for b in range(2):
                V.wait_ge(roots, 4 + b)
                L(V.reciprocal(stat[:, 2 + b:3 + b], stat[:, 2 + b:3 + b]))
                V.scalar_tensor_tensor(hx2[:, b, :], hx2[:, b, :], stat[:, 2 + b:3 + b], finw[:, :], ALU.mult,
                                       ALU.mult).then_inc(fin_ready, 1)


CONSTS = [("ident", P), ("rope", 4 * T), ("dist", 2 * T), ("slot_no", P), ("ident2", CAP), ("desc", 8),
          ("tri", P), ("ones", P), ("selc", 2), ("selm", 8)]
CONST_LOADS = 6
CONST_AT = {}
for _name, _n in CONSTS:
    CONST_AT[_name] = sum(n for m, n in CONSTS[:len(CONST_AT)])
CONST_W = sum(n for _, n in CONSTS)


def constant_table():
    t = np.zeros((P, CONST_W), np.float32)

    def put(name, a):
        a = np.asarray(a, np.float32)
        a = a.reshape(a.shape[0], -1)
        t[:a.shape[0], CONST_AT[name]:CONST_AT[name] + a.shape[1]] = a

    p = np.arange(P)
    put("ident", np.eye(P))
    nf = QK // 4
    inv = np.float32(10000.0) ** (-np.arange(nf, dtype=np.float32) / np.float32(nf))
    tok = np.arange(T)
    ang = np.stack([(tok // GRID).astype(np.float32)[None, :] * inv[p % nf][:, None],
                    (tok % GRID).astype(np.float32)[None, :] * inv[p % nf][:, None]], 1).astype(np.float32)
    sign = np.where(p < nf, 1.0, -1.0)[:, None, None]
    put("rope", np.stack([np.cos(ang), np.sin(ang) * sign], 1))
    put("dist", tok[None, None, :] - (P * np.arange(2)[None, :, None] + p[:, None, None]))
    put("slot_no", np.broadcast_to(p[None, :] % CAP, (P, P)))
    put("ident2", np.concatenate([np.eye(CAP)] * 2))
    put("desc", np.broadcast_to(np.arange(8, 0, -1), (P, 8)))
    put("tri", p[:, None] < p[None, :])
    put("ones", np.ones((P, P)))
    put("selc", [[1, 0], [0, 1], [1, 0], [0, 1], [1, 1]])
    row = np.arange(40)[:, None]
    of = np.arange(8)[None, :]
    put("selm", (row == 4 * of) | (row == 4 * of + 2) | (row == 32 + of))
    return t


_INS = ["x", "c", "ctx", "c_ctx", "w_mod", "b_mod", "norm1_w", "norm2_w", "w_in", "ret_log_decay", "ret_gn_w",
        "w_ret_o", "conv_w", "w_conv_o", "w_out", "router_group_w", "router_group_b", "router_expert_w",
        "router_expert_b", "expert_w13", "expert_w2", "final_norm_w"]


def kernel(**inputs):
    import concourse.bacc as bacc
    from concourse.bass_utils import run_bass_kernel_spmd

    nc = bacc.Bacc("TRN2", target_bir_lowering=False, num_devices=1)
    arrays, args = {}, []
    for name in _INS + ["consts"]:
        a = constant_table() if name == "consts" else np.ascontiguousarray(inputs[name])
        arrays[f"in_{name}"] = a
        args.append(nc.dram_tensor(f"in_{name}", a.shape, mybir.dt.from_np(a.dtype), kind="ExternalInput").ap())
    out = nc.dram_tensor("out_0", (1, T, D), F32, kind="ExternalOutput").ap()
    block_kernel(nc, *args, out)
    r = run_bass_kernel_spmd(nc, [arrays], core_ids=[0])
    return r.results[0]["out_0"]
```
